# Optimizing a Trainium2 kernel written in Bass

```python
import math
import jax, jax.numpy as jnp
from jax import lax
import numpy as np

D_MODEL = 1024
BATCH = 1
SEQ = 256
DEPTH = 2

N_HEADS = 16
QK_NOPE_DIM = 64
QK_ROPE_DIM = 32
QK_DIM = QK_NOPE_DIM + QK_ROPE_DIM
V_HEAD_DIM = 64
Q_LORA_RANK = 384
KV_LORA_RANK = 256
ROPE_THETA = 10000.0
Q_BLOCK = 128
HYENA_WIDTH = 1024
HYENA_ORDER = 2
SHORT_CONV_WIDTH = 3
FILTER_EMB_DIM = 33
FILTER_HIDDEN = 64
DECAY_TARGET = 1e-2
FAST_DECAY_PCT = 0.3
SLOW_DECAY_PCT = 1.5
N_EXPERTS = 16
EC_CAPACITY_FACTOR = 2
EXPERT_FF = 1408
N_BRANCHES = 2
RMS_EPS = 1e-6

COL_Q = 0
COL_KV = COL_Q + Q_LORA_RANK
COL_KROPE = COL_KV + KV_LORA_RANK
COL_HYENA = COL_KROPE + QK_ROPE_DIM
COL_GATE = COL_HYENA + (HYENA_ORDER + 1) * HYENA_WIDTH
IN_COLS = COL_GATE + N_BRANCHES * D_MODEL

kernel_name = "hybrid_mla_hyena_ec_moe_encoder"

def rms_norm(x, w):
    xf = x.astype(jnp.float32)
    y = xf * lax.rsqrt(jnp.mean(xf * xf, axis=-1, keepdims=True) + RMS_EPS)
    return y.astype(x.dtype) * w

def rope_tables(S):
    pos = jnp.arange(S, dtype=jnp.float32)
    inv_freq = ROPE_THETA ** (-jnp.arange(0, QK_ROPE_DIM, 2, dtype=jnp.float32) / QK_ROPE_DIM)
    ang = pos[:, None] * inv_freq[None, :]
    return jnp.cos(ang), jnp.sin(ang)

def apply_rope(t, cos, sin):
    half = QK_ROPE_DIM // 2
    t1, t2 = t[..., :half], t[..., half:]
    c = cos[None, :, None, :].astype(t.dtype)
    s = sin[None, :, None, :].astype(t.dtype)
    return jnp.concatenate([t1 * c - t2 * s, t1 * s + t2 * c], axis=-1)

def block_attention(q, k, v):
    B, S, H, _ = q.shape
    nb = S // Q_BLOCK
    scale = QK_DIM ** -0.5
    qb = q.reshape(B, nb, Q_BLOCK, H, QK_DIM).transpose(1, 0, 2, 3, 4)

    def one_block(q_blk):
        s = jnp.einsum('bqhd,bkhd->bhqk', q_blk, k).astype(jnp.float32) * scale
        p = jax.nn.softmax(s, axis=-1).astype(v.dtype)
        return jnp.einsum('bhqk,bkhd->bqhd', p, v)

    o = lax.map(one_block, qb)
    return o.transpose(1, 0, 2, 3, 4).reshape(B, S, H * V_HEAD_DIM)

def mla_branch(q_lat, kv_lat, k_rope, cos, sin, q_a_norm_w, w_q_b, kv_a_norm_w, w_kv_b, q_norm_w, k_norm_w):
    B, S, _ = q_lat.shape
    q = (rms_norm(q_lat, q_a_norm_w) @ w_q_b).reshape(B, S, N_HEADS, QK_DIM)
    kv = (rms_norm(kv_lat, kv_a_norm_w) @ w_kv_b).reshape(B, S, N_HEADS, QK_NOPE_DIM + V_HEAD_DIM)
    k_nope, v = kv[..., :QK_NOPE_DIM], kv[..., QK_NOPE_DIM:]
    k_rope_h = jnp.broadcast_to(k_rope[:, :, None, :], (B, S, N_HEADS, QK_ROPE_DIM))
    k = jnp.concatenate([k_nope, k_rope_h], axis=-1)
    q = rms_norm(q, q_norm_w)
    k = rms_norm(k, k_norm_w)
    q = jnp.concatenate([q[..., :QK_NOPE_DIM], apply_rope(q[..., QK_NOPE_DIM:], cos, sin)], axis=-1)
    k = jnp.concatenate([k[..., :QK_NOPE_DIM], apply_rope(k[..., QK_NOPE_DIM:], cos, sin)], axis=-1)
    return block_attention(q, k, v)

def hyena_positional_features(L):
    pos = jnp.arange(L, dtype=jnp.float32)
    t = pos / L
    bands = (FILTER_EMB_DIM - 1) // 2
    f = jnp.linspace(1e-4, bands - 1, bands, dtype=jnp.float32)
    w = 2.0 * math.pi * t[:, None] * f[None, :]
    feats = jnp.concatenate([t[:, None], jnp.cos(w), jnp.sin(w)], axis=-1)
    tau = jnp.abs(pos - (L // 2)) / max(L // 2, 1)
    return feats, tau

def implicit_filters(feats, tau, w1, b1, fr1, w2, b2, fr2, w3):
    f32 = jnp.float32
    h = jnp.sin(fr1.astype(f32) * (feats @ w1.astype(f32) + b1.astype(f32)))
    h = jnp.sin(fr2.astype(f32) * (h @ w2.astype(f32) + b2.astype(f32)))
    h = (h @ w3.astype(f32)).reshape(feats.shape[0], HYENA_ORDER, HYENA_WIDTH)
    max_decay = math.log(DECAY_TARGET) / FAST_DECAY_PCT
    min_decay = math.log(DECAY_TARGET) / SLOW_DECAY_PCT
    deltas = jnp.linspace(min_decay, max_decay, HYENA_WIDTH, dtype=f32)
    h = h * jnp.exp(-tau[:, None, None] * jnp.abs(deltas))[:, None, :] if False else h * jnp.exp(-tau[:, None, None] * jnp.abs(deltas)[None, None, :])
    return h / jnp.sum(jnp.abs(h), axis=0, keepdims=True)

def long_conv(z, h_spec, skip):
    L = z.shape[1]
    Z = jnp.fft.rfft(z.astype(jnp.float32), n=2 * L, axis=1)
    y = jnp.fft.irfft(Z * h_spec[None], n=2 * L, axis=1)[:, L // 2: L // 2 + L]
    return y.astype(z.dtype) + z * skip

def short_conv(u, w, b):
    S = u.shape[1]
    pad = SHORT_CONV_WIDTH // 2
    up = jnp.pad(u, ((0, 0), (pad, pad), (0, 0)))
    out = b
    for j in range(SHORT_CONV_WIDTH):
        out = out + up[:, j:j + S] * w[j]
    return out

def hyena_branch(u_cols, feats, tau, conv_w, conv_b, fw1, fb1, ff1, fw2, fb2, ff2, fw3, skip):
    S = u_cols.shape[1]
    u = short_conv(u_cols, conv_w, conv_b)
    parts = jnp.split(u, HYENA_ORDER + 1, axis=-1)
    h = implicit_filters(feats, tau, fw1, fb1, ff1, fw2, fb2, ff2, fw3)
    h_spec = jnp.fft.rfft(h, n=2 * S, axis=0)
    z = parts[0]
    for n in range(HYENA_ORDER):
        z = parts[n + 1] * long_conv(z, h_spec[:, n], skip[n])
    return z

def expert_choice_ffn(h, router_w, wg, wu, wd):
    B, S, D = h.shape
    C = max(1, EC_CAPACITY_FACTOR * S // N_EXPERTS)
    aff = jax.nn.softmax((h @ router_w).astype(jnp.float32), axis=-1)
    gate, idx = lax.top_k(jnp.swapaxes(aff, 1, 2), C)
    flat_idx = idx.reshape(B, N_EXPERTS * C)
    xs = jnp.take_along_axis(h, flat_idx[..., None], axis=1).reshape(B, N_EXPERTS, C, D)
    a = jnp.einsum('becd,edf->becf', xs, wg)
    u = jnp.einsum('becd,edf->becf', xs, wu)
    o = jnp.einsum('becf,efd->becd', jax.nn.silu(a) * u, wd) * gate[..., None].astype(h.dtype)
    o = o.reshape(B, N_EXPERTS * C, D)
    return jax.vmap(lambda oi, ii: jnp.zeros((S, D), h.dtype).at[ii].add(oi))(o, flat_idx)

def setup_inputs(seed: int = 0) -> dict:
    key = jax.random.key(seed)
    ks = jax.random.split(key, 32)

    def nrm(k, shape, scale):
        return jax.random.normal(k, shape, jnp.float32) * scale

    L = DEPTH
    return {
        "x": nrm(ks[0], (BATCH, SEQ, D_MODEL), 1.0),
        "norm1_w": 1.0 + nrm(ks[1], (L, D_MODEL), 0.02),
        "w_in": nrm(ks[2], (L, D_MODEL, IN_COLS), D_MODEL ** -0.5),
        "q_a_norm_w": 1.0 + nrm(ks[3], (L, Q_LORA_RANK), 0.02),
        "w_q_b": nrm(ks[4], (L, Q_LORA_RANK, N_HEADS * QK_DIM), Q_LORA_RANK ** -0.5),
        "kv_a_norm_w": 1.0 + nrm(ks[5], (L, KV_LORA_RANK), 0.02),
        "w_kv_b": nrm(ks[6], (L, KV_LORA_RANK, N_HEADS * (QK_NOPE_DIM + V_HEAD_DIM)), KV_LORA_RANK ** -0.5),
        "q_norm_w": 1.0 + nrm(ks[7], (L, QK_DIM), 0.02),
        "k_norm_w": 1.0 + nrm(ks[8], (L, QK_DIM), 0.02),
        "short_conv_w": nrm(ks[9], (L, SHORT_CONV_WIDTH, (HYENA_ORDER + 1) * HYENA_WIDTH), SHORT_CONV_WIDTH ** -0.5),
        "short_conv_b": nrm(ks[10], (L, (HYENA_ORDER + 1) * HYENA_WIDTH), 0.02),
        "filt_w1": nrm(ks[11], (L, FILTER_EMB_DIM, FILTER_HIDDEN), FILTER_EMB_DIM ** -0.5),
        "filt_b1": nrm(ks[12], (L, FILTER_HIDDEN), 0.1),
        "filt_freq1": 1.0 + nrm(ks[13], (L, FILTER_HIDDEN), 0.02),
        "filt_w2": nrm(ks[14], (L, FILTER_HIDDEN, FILTER_HIDDEN), FILTER_HIDDEN ** -0.5),
        "filt_b2": nrm(ks[15], (L, FILTER_HIDDEN), 0.1),
        "filt_freq2": 1.0 + nrm(ks[16], (L, FILTER_HIDDEN), 0.02),
        "filt_w3": nrm(ks[17], (L, FILTER_HIDDEN, HYENA_ORDER * HYENA_WIDTH), FILTER_HIDDEN ** -0.5),
        "filt_skip": nrm(ks[18], (L, HYENA_ORDER, HYENA_WIDTH), 0.5),
        "w_attn_branch": nrm(ks[19], (L, N_HEADS * V_HEAD_DIM, D_MODEL), (N_HEADS * V_HEAD_DIM) ** -0.5),
        "w_hyena_branch": nrm(ks[20], (L, HYENA_WIDTH, D_MODEL), HYENA_WIDTH ** -0.5),
        "w_out": nrm(ks[21], (L, D_MODEL, D_MODEL), D_MODEL ** -0.5),
        "norm2_w": 1.0 + nrm(ks[22], (L, D_MODEL), 0.02),
        "router_w": nrm(ks[23], (L, D_MODEL, N_EXPERTS), D_MODEL ** -0.5),
        "expert_w_gate": nrm(ks[24], (L, N_EXPERTS, D_MODEL, EXPERT_FF), D_MODEL ** -0.5),
        "expert_w_up": nrm(ks[25], (L, N_EXPERTS, D_MODEL, EXPERT_FF), D_MODEL ** -0.5),
        "expert_w_down": nrm(ks[26], (L, N_EXPERTS, EXPERT_FF, D_MODEL), EXPERT_FF ** -0.5),
    }

def reference(x, norm1_w, w_in, q_a_norm_w, w_q_b, kv_a_norm_w, w_kv_b, q_norm_w, k_norm_w,
              short_conv_w, short_conv_b, filt_w1, filt_b1, filt_freq1, filt_w2, filt_b2, filt_freq2,
              filt_w3, filt_skip, w_attn_branch, w_hyena_branch, w_out, norm2_w, router_w,
              expert_w_gate, expert_w_up, expert_w_down):
    B, S, D = x.shape
    cos, sin = rope_tables(S)
    feats, tau = hyena_positional_features(S)
    for l in range(DEPTH):
        xn = rms_norm(x, norm1_w[l])
        cols = xn @ w_in[l]
        attn = mla_branch(cols[..., COL_Q:COL_KV], cols[..., COL_KV:COL_KROPE],
                          cols[..., COL_KROPE:COL_HYENA], cos, sin,
                          q_a_norm_w[l], w_q_b[l], kv_a_norm_w[l], w_kv_b[l], q_norm_w[l], k_norm_w[l])
        hy = hyena_branch(cols[..., COL_HYENA:COL_GATE], feats, tau, short_conv_w[l], short_conv_b[l],
                          filt_w1[l], filt_b1[l], filt_freq1[l], filt_w2[l], filt_b2[l], filt_freq2[l],
                          filt_w3[l], filt_skip[l])
        gates = jax.nn.sigmoid(cols[..., COL_GATE:].astype(jnp.float32)).astype(x.dtype)
        gates = gates.reshape(B, S, N_BRANCHES, D)
        merged = gates[:, :, 0] * (attn @ w_attn_branch[l]) + gates[:, :, 1] * (hy @ w_hyena_branch[l])
        x = x + merged @ w_out[l]
        x = x + expert_choice_ffn(rms_norm(x, norm2_w[l]), router_w[l],
                                  expert_w_gate[l], expert_w_up[l], expert_w_down[l])
    return x


_drawn_inputs = setup_inputs


def setup_inputs(seed=0):
    import zlib

    import numpy as np

    out = dict(_drawn_inputs(seed))
    spreads = {}
    factors = {'norm1_w': 3.684,
     'q_a_norm_w': 8.0,
     'kv_a_norm_w': 8.0,
     'q_norm_w': 8.0,
     'k_norm_w': 7.042,
     'short_conv_b': 4.441,
     'filt_b1': 3.136,
     'filt_freq1': 8.0,
     'filt_freq2': 8.0,
     'norm2_w': 8.0}
    for name, (base, spread) in spreads.items():
        noise = np.random.default_rng([zlib.crc32(name.encode()), seed]).standard_normal(out[name].shape)
        drawn = base * np.exp(spread * noise) if base else spread * noise
        out[name] = __import__('jax').numpy.asarray(drawn.astype(out[name].dtype))
    for name, factor in factors.items():
        out[name] = (out[name] * factor).astype(out[name].dtype)
    return out
```

```python
from contextlib import ExitStack

import concourse.bass as bass
from concourse import mybir

F32 = mybir.dt.float32
ALU = mybir.AluOpType
ACT = mybir.ActivationFunctionType
AX = mybir.AxisListType
ds = bass.ds

P = 128
D, S, DEPTH = 1024, 256, 2
SB, DB = S // P, D // P
NH, NOPE, ROPE, VD = 16, 64, 32, 64
QK = NOPE + ROPE
HALF = ROPE // 2
QR, KVR = 384, 256
LAT = QR + ROPE + KVR
QB, KVB = QR // P, KVR // P
E, FF = 16, 1408
CAP = 2 * S // E
GROUP = P // CAP
NG = E // GROUP
CT = P // CAP
FT = FF // CT
KF = [P, P, FT - 2 * P]
NF = 384
HW = 512
EPS = 1e-6

FREE = 1

UNIT = DB * 512
NU, RING = 17, 5
UNIT0 = 2048
SLOT = DB * FF
M2AT = DB * LAT


def unit_slot(n):
    return (n + 2) % RING


def uT_block(b):
    return b // 4 % 3 * DB + b // 12 * 4 + b % 4


UNITS_IN_SLOT = [sum(unit_slot(n) == s for n in range(NU)) for s in range(RING)]

C_ID, C_F, C_IF = 0, 128, 128 + SB * NF
C_COS = C_IF + 3 * S
C_SIN = C_COS + SB * HALF
C_IOTA = C_SIN + SB * HALF
C_ONES = C_IOTA + P
C_FEAT = C_ONES + 1
C_EPS = C_FEAT + S
C_N = C_EPS + 1
KSC = QR + KVR
TWO_PI = 6.283185307179586
TWO_PI_PARTS = (6.28125, 0.0019350051879882812, 3.0199159795074593e-07)
ROUND = 12582912.0
PI_BELOW = 3.1415925
V_N1, V_QA, V_KVA = 0, DB, DB + QB
V_CW = V_KVA + KVB
V_CB = V_CW + 3 * 24
V_SKIP = V_CB + 24
V_FB1 = V_SKIP + 16
V_N = V_FB1 + 4
W_N2, W_RT = 0, DB
W_N = DB + DB * E


def build(nc, x_in, vecs, fvecs, qkw_in, consts_in, decay_in, w_lat, w_q_b, units_in,
          filt12, filt3, w_gate, w_up, w_down, out):
    with ExitStack() as ctx:
        def sb(name, cols):
            return ctx.enter_context(nc.sbuf_tensor(name, [P, cols], F32))

        def sem(name):
            return ctx.enter_context(nc.semaphore(name))

        ring = sb("ring", 2 * SLOT)
        R = sb("region", 12 * 1024)
        xt = sb("x", SB * D)
        xnT_t = sb("xnT", DB * S)
        uT_t = sb("uT", 24 * S)
        aT_t = sb("attnT", DB * S)
        W = sb("work", 3072)
        cst = sb("consts", C_N)
        vec = sb("vec", V_N)
        fvec = sb("fvec", W_N)
        qkw = sb("qkw", 2 * QK)
        small = sb("small", 340)
        ps_t = ctx.enter_context(nc.psum_tensor("ps", [P, 8, 512], F32))

        def bank(b, n=512, off=0, rows=P, row0=0):
            return ps_t[row0:row0 + rows, b, off:off + n]

        ident = cst[:, C_ID:C_ID + P]
        x3 = xt[:, :].rearrange("p (b d) -> p b d", b=SB)
        xnT = xnT_t[:, :].rearrange("p (i s) -> p i s", i=DB)
        xn2 = xnT_t[:, :].rearrange("p (b d) -> p b d", b=SB)
        uT = uT_t[:, :].rearrange("p (c s) -> p c s", s=S)
        aT = aT_t[:, :].rearrange("p (i s) -> p i s", s=S)
        xn = R[:, 0:SB * D].rearrange("p (b d) -> p b d", b=SB)
        q_t = R[:, 0:SB * NH * QK].rearrange("p (b c) -> p b c", b=SB)
        q4 = R[:, 0:SB * NH * QK].rearrange("p (b h c) -> p b h c", b=SB, h=NH)
        k0 = SB * NH * QK
        k4 = R[:, k0:2 * k0].rearrange("p (b h c) -> p b h c", b=SB, h=NH)
        v_t = R[:, 2 * k0:2 * k0 + SB * D].rearrange("p (b c) -> p b c", b=SB)
        w3 = R[0:64, 8192:8192 + 2048]
        w12 = R[0:64, 10240:10432]
        h2T = R[0:64, 10432:10432 + S]
        h1T = R[0:64, 10688:10688 + S]
        rr = R[0:64, 10944:10944 + 768]
        habs = R[:, 10688:11712]
        spec = R[:, 0:8192].rearrange("p (n b c) -> p n b c", n=2, b=4)
        z_t = R[:, 8192:10240].rearrange("p (h b c) -> p h b c", h=2, b=SB)
        prod = R[:, 10240:12288].rearrange("p (k c) -> p k c", k=4)
        lat = W[:, 0:SB * LAT].rearrange("p (b c) -> p b c", b=SB)
        latT = W[:, SB * LAT:SB * LAT + 5 * S].rearrange("p (i s) -> p i s", s=S)
        p_t = W[:, 0:1024].rearrange("p (t b k) -> p t b k", t=2, b=SB)
        pT_t = W[:, 1024:2048].rearrange("p (t b k) -> p t b k", t=2, b=SB)
        qkT = W[:, 2048:3072].rearrange("p (t c) -> p t c", t=2)
        decay = W[:, 0:2048].rearrange("p (b c) -> p b c", b=SB)
        hflt = W[:, 2048:3072].rearrange("p (b c) -> p b c", b=SB)
        yT_t = W[:, 0:1536].rearrange("p (b c) -> p b c", b=3)
        prod2 = W[:, 1536:3072].rearrange("p (b c) -> p b c", b=3)
        sg = W[:, 0:1024].rearrange("p (t c) -> p t c", t=2)
        gm_t = W[:, 1024:2048].rearrange("p (t c) -> p t c", t=2)
        qsq = uT_t[:, 3072:6144].rearrange("p (b h c) -> p b h c", b=SB, h=NH)
        ksq = aT_t[:, :].rearrange("p (b h c) -> p b h c", b=SB, h=NH)
        rpA = uT_t[:, 3072:3584].rearrange("p (h t c) -> p h t c", h=NH, t=2)
        rpB = uT_t[:, 3584:4096].rearrange("p (h t c) -> p h t c", h=NH, t=2)
        mT = uT_t[:, 2048:4096].rearrange("p (i s) -> p i s", s=S)
        xs = uT_t[:, 0:1024].rearrange("p (i c) -> p i c", i=DB)
        o_sb = uT_t[:, 1024:2048]
        pick = uT_t[:, 2048:2304].rearrange("p (b c) -> p b c", b=SB)
        gsel = uT_t[:, 2304:2560].rearrange("p (b c) -> p b c", b=SB)
        gselT = uT_t[:, 2560:2816]
        sil = uT_t[:, 2816:2816 + FT]
        hid_e = uT_t[:, 3200:3200 + FT]
        hT = uT_t[:, 3584:3584 + 3 * P]
        lgT = uT_t[0:E, 4096:4096 + S]
        work = uT_t[0:E, 4352:4352 + S]
        rank = uT_t[0:E, 4608:4608 + S]
        picked = uT_t[0:E, 4864:4864 + S]
        ptok = uT_t[0:E, 5120:5120 + S]
        top8 = uT_t[0:E, 5376:5384]
        aff = uT_t[:, 5400:5400 + SB * E].rearrange("p (b e) -> p b e", b=SB)
        pos = uT_t[:, 5440:5440 + SB * E].rearrange("p (b e) -> p b e", b=SB)
        ones = cst[:, C_ONES:C_ONES + 1]

        n1 = small[:, 0:4]
        lr = small[:, 4:12]
        ssqk = small[:, 12:76]
        rqk = small[:, 76:140]
        kr = small[:, 140:204].rearrange("p (b t c) -> p b t c", b=SB, t=2)
        krA = small[:, 204:268].rearrange("p (b t c) -> p b t c", b=SB, t=2)
        kss = small[:, 268:270]
        nmax = small[:, 270:274]
        rsum = small[:, 274:278]
        n2 = small[:, 278:282]
        lmax = small[:, 282:286]
        kt = small[:, 286:288]
        hsum, hinv, hskip = small[:, 288:304], small[:, 304:320], small[:, 320:336]
        krB = uT_t[:, 2600:2664].rearrange("p (b t c) -> p b t c", b=SB, t=2)
        qsq_rows = uT_t[:, 3072:6144].rearrange("p (r c) -> p r c", c=QK)
        ksq_rows = aT_t[:, :].rearrange("p (r c) -> p r c", c=NOPE)
        pos_flat = uT_t[:, 5440:5440 + SB * E]

        m1 = ring[:, 0:M2AT].rearrange("p (i c) -> p i c", i=DB)
        m2 = ring[:, M2AT:M2AT + QB * NH * QK].rearrange("p (i c) -> p i c", i=QB)

        def unit(n):
            a = UNIT0 + unit_slot(n) * UNIT
            return ring[:, a:a + UNIT]

        def unit8(n):
            return unit(n).rearrange("p (i c) -> p i c", i=DB)

        wkv = unit(0).rearrange("p (i c) -> p i c", i=KVB)
        wg = ring[:, 0:SLOT].rearrange("p (i f) -> p i f", i=DB)
        wu = ring[:, SLOT:2 * SLOT].rearrange("p (i f) -> p i f", i=DB)
        wd = R[:, :].rearrange("p (j b d) -> p j b d", j=CT, b=3)

        names = """x_in consts_in vec_in fvec_in qkw_in filt_in decay_in wlat_in wqb_in wg_in wu_in wd_in out_done
        norm1_rms xn_ready xnT_psum xnT_dve xnT_act lat_psum lat_rms lat_ready latT_psum latT_dve latT_act
        filt_psum arg_dve sin_act q_psum q_act kv_psum kv_dve ksq_act qkss_dve qkrms_act qw_pool qkw_scaled qk_ready
        proj_psum conv_act conv_dve
        qkT_psum qkT_act score_psum max_dve exp_act p_dve pT_psum pT_dve pv_psum oT_act
        f3_psum h_dve habs_act dft_psum hsum_psum spec_dve swap_act
        zT_psum z_act zf_psum prod_dve shift_act yf_dve y_psum post_dve
        gate_psum branch_psum sig_act merged_dve
        wout_psum xmid_dve norm2_rms xn2_dve xn2T_psum xn2T_dve xn2T_act lgT_psum lgT_dve lg_psum lmax_dve lexp_act
        aff_dve affT_psum pos_dve pos_psum
        pick_dve xs_psum xs_dve gsel_dve gselT_psum gselT_act gate_done up_done sil_act hid_dve hT_psum hT_dve
        o_psum o_act o_dve y2_psum x_dve""".split()
        s = {n: sem(n) for n in names}
        unit_in = [sem(f"unit_in{i}") for i in range(RING)]
        block = ctx.enter_context(nc.Block())

        @block.sync
        def _(sp):
            sp.dma_start(cst[:, :], consts_in).then_inc(s["consts_in"], 16)
            sp.dma_start(x3, x_in.rearrange("a (b p) d -> p (a b) d", p=P)).then_inc(s["x_in"], 16)
            with sp.Fori(0, DEPTH) as L:
                def unit_is_used(n):
                    if n == 0:
                        sp.wait_ge(s["kv_psum"], (L + 1) * 8)
                    elif n < 7:
                        sp.wait_ge(s["proj_psum"], L * 24 + 4 * n)
                    elif n < 15:
                        sp.wait_ge(s["branch_psum"], L * 8 + (4 if n < 11 else 8))
                    else:
                        sp.wait_ge(s["wout_psum"], L * 4 + 2 * (n - 14))

                sp.wait_ge(s["post_dve"], L * 4 + FREE)
                sp.dma_start(vec[:, :], vecs[L]).then_inc(s["vec_in"], 16)
                sp.dma_start(qkw[:, :], qkw_in[ds(L, 1), :].to_broadcast([P, 2 * QK])).then_inc(s["qkw_in"], 16)
                sp.wait_ge(s["gate_done"], L * E + FREE)
                sp.dma_start(ring[:, 0:M2AT], w_lat[L]).then_inc(s["wlat_in"], 16)
                sp.dma_start(m2, w_q_b[L].rearrange("(i p) c -> p i c", p=P)).then_inc(s["wqb_in"], 16)
                sp.wait_ge(s["up_done"], L * E + FREE)
                sp.dma_start(unit(0), units_in[L, 0]).then_inc(unit_in[unit_slot(0)], 16)
                sp.wait_ge(s["o_psum"], L * E + FREE)
                sp.dma_start(w12, filt12[L]).then_inc(s["filt_in"], 16)
                sp.dma_start(w3, filt3[L]).then_inc(s["filt_in"], 16)
                sp.wait_ge(s["xs_dve"], L * NG + FREE)
                sp.dma_start(fvec[:, :], fvecs[L]).then_inc(s["fvec_in"], 16)
                for n in range(1, NU):
                    if n == 3:
                        sp.wait_ge(s["q_psum"], (L + 1) * 6)
                    if n >= RING:
                        unit_is_used(n - RING)
                    sp.dma_start(unit(n), units_in[L, n]).then_inc(unit_in[unit_slot(n)], 16)

                def load_gate(e):
                    sp.dma_start(wg, w_gate[L * E + e].rearrange("(i p) f -> p i f", p=P)).then_inc(s["wg_in"], 16)

                def load_up(e):
                    sp.dma_start(wu, w_up[L * E + e].rearrange("(i p) f -> p i f", p=P)).then_inc(s["wu_in"], 16)

                def load_down(e):
                    w = w_down[L * E + e].rearrange("(j f) d -> f j d", j=CT)
                    sp.dma_start(wd[:, :, 0, :], w[0:P]).then_inc(s["wd_in"], 16)
                    sp.dma_start(wd[:, :, 1, :], w[P:2 * P]).then_inc(s["wd_in"], 16)
                    sp.dma_start(wd[0:KF[2], :, 2, :], w[2 * P:FT]).then_inc(s["wd_in"], 16)

                sp.wait_ge(s["post_dve"], (L + 1) * 4 + FREE)
                load_down(0)
                unit_is_used(15)
                load_gate(0)
                unit_is_used(16)
                load_up(0)
                with sp.Fori(1, E) as e:
                    sp.wait_ge(s["gate_done"], L * E + e + FREE)
                    load_gate(e)
                    sp.wait_ge(s["up_done"], L * E + e + FREE)
                    load_up(e)
                    sp.wait_ge(s["o_psum"], L * E + e + FREE)
                    load_down(e)
            sp.wait_ge(s["x_dve"], DEPTH * E * 4 + FREE)
            sp.dma_start(out.rearrange("a (b p) d -> p (a b) d", p=P), x3).then_inc(s["out_done"], 16)
            sp.wait_ge(s["out_done"], 16)

        @block.gpsimd
        def _(pool):
            with pool.Fori(0, DEPTH) as L:
                pool.wait_ge(s["qkw_scaled"], L + 1)
                for b in range(SB):
                    pool.wait_ge(s["q_act"], L * 6 + 3 * (b + 1))
                    nc.gpsimd.tensor_tensor(
                        q4[:, b], q4[:, b], qkw[:, 0:QK].unsqueeze(1).to_broadcast([P, NH, QK]),
                        ALU.mult).then_inc(s["qw_pool"], 1)

        @block.tensor
        def _(pe):
            mm = nc.tensor.matmul
            tp = nc.tensor.transpose

            for n in ("gate_done", "up_done", "o_psum"):
                pe.sem_inc(s[n], FREE)
            with pe.Fori(0, DEPTH) as L:
                pe.wait_ge(s["consts_in"], 16)
                pe.wait_ge(s["xn_ready"], L + 1)
                for b in range(4):
                    for c in range(4):
                        i, t = 2 * b + c // 2, c % 2
                        m = tp(bank(b, P, c * P), xn[:, t, i * P:(i + 1) * P], ident)
                    m.then_inc(s["xnT_psum"], 1)
                pe.wait_ge(s["consts_in"], 16)
                pe.wait_ge(s["filt_in"], 32 * (L + 1))
                mm(bank(7, S), w12[0:33, 0:P], cst[0:33, C_FEAT:C_FEAT + S],
                   start=True, stop=True).then_inc(s["filt_psum"], 1)
                pe.wait_ge(s["wlat_in"], 16 * (L + 1))
                pe.wait_ge(s["xnT_dve"], 2 * (L + 1))
                pe.wait_ge(s["xnT_act"], 2 * (L + 1))
                for t in range(SB):
                    for i in range(DB):
                        mm(bank(3 + 2 * t, QR + ROPE), xnT[:, i, t * P:(t + 1) * P], m1[:, i, 0:QR + ROPE],
                           start=i == 0, stop=i == DB - 1)
                    for i in range(DB):
                        m = mm(bank(4 + 2 * t, KVR), xnT[:, i, t * P:(t + 1) * P], m1[:, i, QR + ROPE:LAT],
                               start=i == 0, stop=i == DB - 1)
                m.then_inc(s["lat_psum"], 1)
                blocks = iter(range(24))

                def next_block():
                    b = next(blocks)
                    n, j = 1 + b // 4, b % 4
                    if j == 0:
                        pe.wait_ge(unit_in[unit_slot(n)],
                                   16 * (L * UNITS_IN_SLOT[unit_slot(n)] + n // RING + 1))
                    if b >= 2:
                        pe.wait_ge(s["conv_dve"], L * 24 + b - 1)
                    half_block(b, 0)

                    def rest():
                        half_block(b, 1).then_inc(s["proj_psum"], 1)
                    return rest

                def half_block(b, k):
                    n, j = 1 + b // 4, b % 4
                    for i in range(4 * k, 4 * k + 4):
                        m = mm(bank(b % 2, S), unit8(n)[:, i, j * P:(j + 1) * P], xnT[:, i],
                               start=i == 0, stop=i == DB - 1)
                    return m

                next_block()()
                next_block()()
                pe.wait_ge(s["consts_in"], 16)
                pe.wait_ge(s["sin_act"], 2 * L + 1)
                mm(bank(7, S), w12[:, 64:64 + P], h1T, start=True, stop=True).then_inc(s["filt_psum"], 1)
                pe.wait_ge(s["lat_ready"], L + 1)
                for i in range(5):
                    c0 = i * P if i < QB else QR + ROPE + (i - QB) * P
                    for t in range(SB):
                        m = tp(bank(2 + i // 2, P, (i % 2) * S + t * P), lat[:, t, c0:c0 + P], ident)
                    if i % 2 or i == 4:
                        m.then_inc(s["latT_psum"], 1)
                pe.wait_ge(s["wqb_in"], 16 * (L + 1))
                pe.wait_ge(s["latT_dve"], 2 * (L + 1))
                pe.wait_ge(s["latT_act"], L + 1)
                for g in range(6):
                    t, c = g // 3, g % 3
                    if g >= 4:
                        pe.wait_ge(s["conv_dve"], L * 24 + g - 3)
                    for i in range(QB):
                        m = mm(bank((3 + g) % 7), latT[:, i, t * P:(t + 1) * P], m2[:, i, c * 512:(c + 1) * 512],
                               start=i == 0, stop=i == QB - 1)
                    m.then_inc(s["q_psum"], 1)
                pe.wait_ge(unit_in[unit_slot(0)], 16 * (L * UNITS_IN_SLOT[unit_slot(0)] + 1))
                for g in range(8):
                    t, c = g // 4, g % 4
                    if g < 6:
                        pe.wait_ge(s["q_act"], L * 6 + g + 1)
                    else:
                        pe.wait_ge(s["kv_dve"], L * 8 + g - 5)
                    for i in range(KVB):
                        m = mm(bank((3 + g % 6) % 7), latT[:, QB + i, t * P:(t + 1) * P], wkv[:, i, c * 512:(c + 1) * 512],
                               start=i == 0, stop=i == KVB - 1)
                    m.then_inc(s["kv_psum"], 1)
                pe.wait_ge(s["kv_dve"], (L + 1) * 8)

                for _ in range(6):
                    next_block()()
                pe.wait_ge(s["qk_ready"], L + 1)
                for h in range(NH + 1):
                    if h < NH:
                        if h >= 1:
                            pe.wait_ge(s["qkT_act"], L * NH + h)
                        for w, src in enumerate((q4, k4)):
                            for t in range(SB):
                                m = tp(bank(2, P, w * S + t * P, rows=QK), src[:, t, h], ident)
                        m.then_inc(s["qkT_psum"], 1)
                        rest_of_block = next_block()
                        pe.wait_ge(s["qkT_act"], L * NH + h + 1)
                        if h >= 2:
                            pe.wait_ge(s["exp_act"], L * NH + h - 1)
                        for t in range(SB):
                            m = mm(bank(3 + h % 2, S, t * S), qkT[0:QK, h % 2, t * P:(t + 1) * P],
                                   qkT[0:QK, h % 2, S:2 * S], start=True, stop=True)
                        m.then_inc(s["score_psum"], 1)
                    if h >= 1:
                        g = h - 1
                        pe.wait_ge(s["p_dve"], L * NH + g + 1)
                        if g >= 2:
                            pe.wait_ge(s["pT_dve"], L * NH + g - 1)
                        for kb in range(SB):
                            for t in range(SB):
                                m = tp(bank(5 + g % 2, P, kb * S + t * P), p_t[:, g % 2, t, kb * P:(kb + 1) * P], ident)
                        m.then_inc(s["pT_psum"], 1)
                    if h < NH:
                        rest_of_block()
                    if h >= 1:
                        pe.wait_ge(s["pT_dve"], L * NH + g + 1)
                        if g % 2 == 0 and g >= 2:
                            pe.wait_ge(s["oT_act"], L * (NH // 2) + g // 2)
                        for kb in range(SB):
                            m = mm(bank(7, S, rows=VD, row0=VD * (g % 2)), v_t[:, kb, g * VD:(g + 1) * VD],
                                   pT_t[:, g % 2, kb], start=kb == 0, stop=kb == SB - 1)
                        m.then_inc(s["pv_psum"], 1)
                pe.wait_ge(s["conv_dve"], (L + 1) * 24)
                pe.wait_ge(s["oT_act"], (L + 1) * (NH // 2))

                def filter_time(it):
                    n, c = it // 2, it % 2
                    if it == 0:
                        pe.wait_ge(s["sin_act"], 2 * L + 2)
                    if it >= 2:
                        pe.wait_ge(s["h_dve"], L * 4 + it - 1)
                    for t in range(SB):
                        m = mm(bank(2 * (it % 2) + t), h2T[:, t * P:(t + 1) * P],
                               w3[:, n * D + c * HW:n * D + (c + 1) * HW], start=True, stop=True)
                    m.then_inc(s["f3_psum"], 1)

                filter_time(0)
                for it in range(4):
                    if it < 3:
                        filter_time(it + 1)
                    pe.wait_ge(s["h_dve"], L * 4 + it + 1)
                    if it >= 1:
                        pe.wait_ge(s["spec_dve"], L * 16 + 4 * it)
                    for f in range(3):
                        for t in range(SB):
                            m = mm(bank(5 + f), cst[:, C_F + t * NF + f * P:C_F + t * NF + (f + 1) * P],
                                   hflt[:, t], start=t == 0, stop=t == SB - 1)
                    m.then_inc(s["dft_psum"], 1)
                    pe.wait_ge(s["habs_act"], L * 4 + it + 1)
                    for j in range(4):
                        for t in range(SB):
                            m = mm(bank(4, 1, j), habs[:, t * HW + j * P:t * HW + (j + 1) * P], ones,
                                   start=t == 0, stop=t == SB - 1)
                    m.then_inc(s["hsum_psum"], 1)
                pe.wait_ge(s["spec_dve"], (L + 1) * 16)

                def to_spectrum(it):
                    n, c = it // 2, it % 2
                    if it >= 2:
                        pe.wait_ge(s["post_dve"], L * 4 + it - 1 + FREE)
                    if it >= 1:
                        pe.wait_ge(s["z_act"], L * 4 + it)
                    for t in range(SB):
                        for j in range(4):
                            m = tp(bank(t, P, j * P), uT[:, 4 * c + j, t * P:(t + 1) * P], ident)
                    m.then_inc(s["zT_psum"], 1)
                    pe.wait_ge(s["z_act"], L * 4 + it + 1)
                    if it >= 1:
                        pe.wait_ge(s["prod_dve"], L * 4 + it)
                    for f in range(3):
                        for t in range(SB):
                            m = mm(bank(2 + f), cst[:, C_F + t * NF + f * P:C_F + t * NF + (f + 1) * P],
                                   z_t[:, c, t], start=t == 0, stop=t == SB - 1)
                    m.then_inc(s["zf_psum"], 1)

                def from_spectrum(it):
                    pe.wait_ge(s["yf_dve"], L * 4 + it + 1)
                    if it >= 1:
                        pe.wait_ge(s["post_dve"], L * 4 + it + FREE)
                    for j in range(4):
                        for f in range(3):
                            m = mm(bank(5 + j // 2, S, (j % 2) * S), yT_t[:, f, j * P:(j + 1) * P],
                                   cst[:, C_IF + f * S:C_IF + (f + 1) * S], start=f == 0, stop=f == 2)
                        if j % 2:
                            m.then_inc(s["y_psum"], 1)

                to_spectrum(0)
                for it in range(4):
                    if it < 3:
                        to_spectrum(it + 1)
                    from_spectrum(it)
                pe.wait_ge(s["post_dve"], (L + 1) * 4 + FREE)

                for i in range(DB):
                    c, j = i // 4, i % 4
                    for g in range(4):
                        n = 7 + 4 * c + g
                        if j == 0:
                            pe.wait_ge(unit_in[unit_slot(n)],
                                       16 * (L * UNITS_IN_SLOT[unit_slot(n)] + n // RING + 1))
                        if g == 0 and i >= 2:
                            pe.wait_ge(s["sig_act"], L * 8 + i - 1)
                        if g == 2 and i >= 2:
                            pe.wait_ge(s["merged_dve"], L * 8 + i - 1)
                        src = (xnT, xnT, aT, uT)[g]
                        for k in range(DB):
                            m = mm(bank(2 * (i % 2) + g // 2, S, (g % 2) * S), unit8(n)[:, k, j * P:(j + 1) * P],
                                   src[:, k], start=k == 0, stop=k == DB - 1)
                        if g == 1:
                            m.then_inc(s["gate_psum"], 1)
                        if g == 3:
                            m.then_inc(s["branch_psum"], 1)
                pe.wait_ge(s["merged_dve"], (L + 1) * 8)
                for c in range(2):
                    n = 15 + c
                    pe.wait_ge(unit_in[unit_slot(n)], 16 * (L * UNITS_IN_SLOT[unit_slot(n)] + n // RING + 1))
                    for t in range(SB):
                        for k in range(DB):
                            m = mm(bank(4 + 2 * c + t), mT[:, k, t * P:(t + 1) * P], unit8(n)[:, k],
                                   start=k == 0, stop=k == DB - 1)
                        m.then_inc(s["wout_psum"], 1)
                pe.wait_ge(s["xn2_dve"], L + 1)
                for b in range(4):
                    for c in range(4):
                        i, t = 2 * b + c // 2, c % 2
                        m = tp(bank(b, P, c * P), xn2[:, t, i * P:(i + 1) * P], ident)
                    m.then_inc(s["xn2T_psum"], 1)
                pe.wait_ge(s["fvec_in"], 16 * (L + 1))
                pe.wait_ge(s["xn2T_dve"], 2 * (L + 1))
                pe.wait_ge(s["xn2T_act"], 2 * (L + 1))
                for i in range(DB):
                    m = mm(bank(4, S, rows=E), fvec[:, W_RT + i * E:W_RT + (i + 1) * E], aT[:, i],
                           start=i == 0, stop=i == DB - 1)
                m.then_inc(s["lgT_psum"], 1)
                pe.wait_ge(s["consts_in"], 16)
                pe.wait_ge(s["lgT_dve"], L + 1)
                for t in range(SB):
                    m = tp(bank(5, E, t * E), lgT[:, t * P:(t + 1) * P], ident[0:E, 0:E])
                m.then_inc(s["lg_psum"], 1)
                pe.wait_ge(s["aff_dve"], L + 1)
                for t in range(SB):
                    m = tp(bank(6, P, t * P, rows=E), aff[:, t], ident)
                m.then_inc(s["affT_psum"], 1)
                pe.wait_ge(s["consts_in"], 16)
                pe.wait_ge(s["pos_dve"], L + 1)
                for t in range(SB):
                    m = tp(bank(7, E, t * E), ptok[:, t * P:(t + 1) * P], ident[0:E, 0:E])
                m.then_inc(s["pos_psum"], 1)

                with pe.Fori(0, NG) as g:
                    pe.wait_ge(s["pick_dve"], L * NG + g + 1)
                    pe.wait_ge(s["o_act"], L * E + g * GROUP + FREE)
                    pe.wait_ge(s["o_dve"], L * E + g * GROUP + FREE)
                    for i in range(DB):
                        for t in range(SB):
                            m = mm(bank(i // 4, P, (i % 4) * P), xn2[:, t, i * P:(i + 1) * P], pick[:, t],
                                   start=t == 0, stop=t == SB - 1)
                    m.then_inc(s["xs_psum"], 1)
                    pe.wait_ge(s["xs_dve"], L * NG + g + 1 + FREE)
                    for q in range(GROUP):
                        n = L * E + g * GROUP + q
                        for w, b, arrived, read, done in ((wg, 2, "wg_in", "sil_act", "gate_done"),
                                                          (wu, 3, "wu_in", "hid_dve", "up_done")):
                            pe.wait_ge(s[arrived], 16 * n + 16)
                            pe.wait_ge(s[read], n + FREE)
                            for i in range(DB):
                                for j in range(CT):
                                    m = mm(bank(b, FT, rows=CAP, row0=CAP * j), xs[:, i, q * CAP:(q + 1) * CAP],
                                           w[:, i, j * FT:(j + 1) * FT], start=i == 0, stop=i == DB - 1)
                            m.then_inc(s[done], 1)
                        pe.wait_ge(s["gsel_dve"], n + 1)
                        for t in range(SB):
                            m = tp(bank(4, P, t * P), gsel[:, t], ident)
                        m.then_inc(s["gselT_psum"], 1)
                        pe.wait_ge(s["hid_dve"], n + 1 + FREE)
                        for b in range(3):
                            m = tp(bank(5, P, b * P, rows=KF[b]), hid_e[:, b * P:b * P + KF[b]], ident)
                        m.then_inc(s["hT_psum"], 1)
                        pe.wait_ge(s["wd_in"], 48 * n + 48)
                        pe.wait_ge(s["hT_dve"], n + 1)
                        pe.wait_ge(s["o_act"], n + FREE)
                        pe.wait_ge(s["o_dve"], n + FREE)
                        for c in range(2):
                            for b in range(3):
                                for j in range(CT):
                                    m = mm(bank(c, rows=CAP, row0=CAP * j),
                                           hT[0:KF[b], b * P + CAP * j:b * P + CAP * (j + 1)],
                                           wd[0:KF[b], j, b, c * 512:(c + 1) * 512], start=b == 0, stop=b == 2)
                        m.then_inc(s["o_psum"], 1)
                        pe.wait_ge(s["gselT_act"], n + 1)
                        for k in range(4):
                            t, c = k // 2, k % 2
                            if k == 0:
                                pe.wait_ge(s["o_act"], n + 1 + FREE)
                            if k == 1:
                                pe.wait_ge(s["o_dve"], n + 1 + FREE)
                            pe.wait_ge(s["x_dve"], n * 4 + max(k - 1, 0) + FREE)
                            mm(bank(6 + k % 2), gselT[:, t * P:(t + 1) * P], o_sb[:, c * 512:(c + 1) * 512],
                               start=True, stop=True).then_inc(s["y2_psum"], 1)

        @block.scalar
        def _(act):
            af = nc.scalar.activation

            def conv(L, b):
                ch = uT_block(b)
                act.wait_ge(s["proj_psum"], L * 24 + b + 1)
                af(uT[:, ch], bank(b % 2, S), ACT.Identity, bias=vec[:, V_CB + ch:V_CB + ch + 1],
                   scale=vec[:, V_CW + 24 + ch:V_CW + 25 + ch]).then_inc(s["conv_act"], 1)

            act.wait_ge(s["x_in"], 16)
            act.wait_ge(s["consts_in"], 16)
            eps = cst[:, C_EPS:C_EPS + 1]
            for n in ("sil_act", "o_act"):
                act.sem_inc(s[n], FREE)
            with act.Fori(0, DEPTH) as L:
                act.wait_ge(s["x_dve"], L * E * 4 + FREE)
                for t in range(SB):
                    af(W[:, t * D:(t + 1) * D], x3[:, t], ACT.Square, accum_out=n1[:, t:t + 1])
                act.drain()
                af(n1[:, 2:4], n1[:, 0:2], ACT.Sqrt, bias=eps, scale=1.0 / D).then_inc(s["norm1_rms"], 1)
                act.wait_ge(s["vec_in"], 16 * (L + 1))
                for b in (1, 3):
                    act.wait_ge(s["xnT_psum"], L * 4 + b + 1)
                    for i in (2 * b, 2 * b + 1):
                        m = af(xnT[:, i], bank(b, S, (i % 2) * S), ACT.Copy, scale=vec[:, V_N1 + i:V_N1 + i + 1])
                    m.then_inc(s["xnT_act"], 1)
                act.wait_ge(s["arg_dve"], 2 * L + 1)
                af(h1T, rr[:, 2 * S:3 * S], ACT.Sin).then_inc(s["sin_act"], 1)
                act.wait_ge(s["lat_psum"], L + 1)
                for t in range(SB):
                    af(uT_t[:, t * KSC:t * KSC + QR], bank(3 + 2 * t, QR), ACT.Square, accum_out=lr[:, t:t + 1])
                    af(uT_t[:, t * KSC + QR:t * KSC + QR + KVR], bank(4 + 2 * t, KVR), ACT.Square,
                       accum_out=lr[:, 2 + t:3 + t])
                act.drain()
                af(lr[:, 4:6], lr[:, 0:2], ACT.Sqrt, bias=eps, scale=1.0 / QR)
                af(lr[:, 6:8], lr[:, 2:4], ACT.Sqrt, bias=eps, scale=1.0 / KVR).then_inc(s["lat_rms"], 1)
                conv(L, 0)
                act.wait_ge(s["latT_psum"], L * 3 + 2)
                af(latT[:, 2], bank(3, S), ACT.Copy, scale=vec[:, V_QA + 2:V_QA + 3])
                af(latT[:, 3], bank(3, S, S), ACT.Copy, scale=vec[:, V_KVA:V_KVA + 1]).then_inc(s["latT_act"], 1)
                conv(L, 1)
                act.wait_ge(s["arg_dve"], 2 * L + 2)
                af(h2T, rr[:, 2 * S:3 * S], ACT.Sin).then_inc(s["sin_act"], 1)
                qsq_flat = uT_t[:, 3072:6144]
                for g in range(6):
                    t, c = g // 3, g % 3
                    act.wait_ge(s["q_psum"], L * 6 + g + 1)
                    af(qsq_flat[:, g * 512:(g + 1) * 512], bank((3 + g) % 7), ACT.Square)
                    af(q_t[:, t, c * 512:(c + 1) * 512], bank((3 + g) % 7), ACT.Copy).then_inc(s["q_act"], 1)
                for t in range(SB):
                    act.wait_ge(s["kv_dve"], L * 8 + 4 * t + 2)
                    af(ksq[:, t], k4[:, t, :, 0:NOPE], ACT.Square).then_inc(s["ksq_act"], 1)
                conv(L, 2)
                conv(L, 3)
                act.wait_ge(s["qkss_dve"], L + 1)
                af(rqk[:, :], ssqk[:, :], ACT.Sqrt, bias=eps, scale=1.0 / QK).then_inc(s["qkrms_act"], 1)
                blocks = iter(range(4, 24))
                for _ in range(4):
                    conv(L, next(blocks))
                for h in range(NH + 1):
                    if h < NH:
                        act.wait_ge(s["qkT_psum"], L * NH + h + 1)
                        af(qkT[0:QK, h % 2], bank(2, rows=QK), ACT.Copy).then_inc(s["qkT_act"], 1)
                        act.wait_ge(s["max_dve"], L * NH + h + 1)
                        for t in range(SB):
                            c = 2 * (h % 2) + t
                            m = af(p_t[:, h % 2, t], bank(3 + h % 2, S, t * S), ACT.Exp, bias=nmax[:, c:c + 1],
                                   accum_out=rsum[:, c:c + 1])
                        m.then_inc(s["exp_act"], 1)
                        conv(L, next(blocks))
                    if h >= 1 and h % 2 == 0:
                        g = h - 1
                        act.wait_ge(s["pv_psum"], L * NH + g + 1)
                        af(aT[:, g // 2], bank(7, S), ACT.Copy).then_inc(s["oT_act"], 1)
                act.dma_start(decay, decay_in).then_inc(s["decay_in"], 16)
                def abs_h(it):
                    act.wait_ge(s["h_dve"], L * 4 + it + 1)
                    if it >= 1:
                        act.wait_ge(s["hsum_psum"], L * 4 + it)
                    af(habs, W[:, 2048:3072], ACT.Abs).then_inc(s["habs_act"], 1)

                abs_h(0)
                for it in range(4):
                    n, c = it // 2, it % 2
                    if it < 3:
                        abs_h(it + 1)
                    act.wait_ge(s["spec_dve"], L * 16 + 4 * it + 1)
                    cs = slice(c * HW, (c + 1) * HW)
                    af(spec[0:64, n, 3, cs], spec[64:128, n, 2, cs], ACT.Copy)
                    af(spec[64:128, n, 3, cs], spec[0:64, n, 2, cs], ACT.Copy).then_inc(s["swap_act"], 1)

                def z_out(it):
                    act.wait_ge(s["zT_psum"], L * 4 + it + 1)
                    for t in range(SB):
                        m = af(z_t[:, it % 2, t], bank(t), ACT.Copy)
                    m.then_inc(s["z_act"], 1)

                z_out(0)
                z_out(1)
                for it in range(4):
                    if it >= 2:
                        z_out(it)
                    act.wait_ge(s["prod_dve"], L * 4 + it + 1)
                    af(prod2[0:64, 2], prod2[64:128, 0], ACT.Copy)
                    af(prod2[64:128, 2], prod2[0:64, 1], ACT.Copy).then_inc(s["shift_act"], 1)
                for i in range(DB):
                    act.wait_ge(s["gate_psum"], L * 8 + i + 1)
                    if i >= 2:
                        act.wait_ge(s["merged_dve"], L * 8 + i - 1)
                    af(sg[:, i % 2], bank(2 * (i % 2)), ACT.Sigmoid).then_inc(s["sig_act"], 1)
                act.wait_ge(s["xmid_dve"], L + 1)
                for t in range(SB):
                    af(W[:, t * D:(t + 1) * D], x3[:, t], ACT.Square, accum_out=n2[:, t:t + 1])
                act.drain()
                af(n2[:, 2:4], n2[:, 0:2], ACT.Sqrt, bias=eps, scale=1.0 / D).then_inc(s["norm2_rms"], 1)
                act.wait_ge(s["fvec_in"], 16 * (L + 1))
                for b in (1, 3):
                    act.wait_ge(s["xn2T_psum"], L * 4 + b + 1)
                    for i in (2 * b, 2 * b + 1):
                        m = af(aT[:, i], bank(b, S, (i % 2) * S), ACT.Copy, scale=fvec[:, W_N2 + i:W_N2 + i + 1])
                    m.then_inc(s["xn2T_act"], 1)
                act.wait_ge(s["lmax_dve"], L + 1)
                for t in range(SB):
                    m = af(aff[:, t], bank(5, E, t * E), ACT.Exp, bias=lmax[:, t:t + 1],
                           accum_out=lmax[:, 2 + t:3 + t])
                m.then_inc(s["lexp_act"], 1)
                with act.Fori(0, E) as e:
                    n = L * E + e
                    act.wait_ge(s["gate_done"], n + 1 + FREE)
                    act.wait_ge(s["hid_dve"], n + FREE)
                    af(sil, bank(2, FT), ACT.Silu).then_inc(s["sil_act"], 1)
                    act.wait_ge(s["gselT_psum"], n + 1)
                    af(gselT, bank(4, S), ACT.Copy).then_inc(s["gselT_act"], 1)
                    act.wait_ge(s["o_psum"], n + 1 + FREE)
                    af(o_sb[:, 0:512], bank(0), ACT.Copy).then_inc(s["o_act"], 1)

        @block.vector
        def _(dve):
            tt, ts, stt = nc.vector.tensor_tensor, nc.vector.tensor_scalar, nc.vector.scalar_tensor_tensor
            recip, copy, reduce = nc.vector.reciprocal, nc.vector.tensor_copy, nc.vector.tensor_reduce

            def conv(L, b):
                ch = uT_block(b)
                dve.wait_ge(s["conv_act"], L * 24 + b + 1)
                pb = b % 2
                stt(uT[:, ch, 1:S], bank(pb, S - 1), vec[:, V_CW + ch:V_CW + ch + 1], uT[:, ch, 1:S],
                    ALU.mult, ALU.add)
                dve.drain()
                stt(uT[:, ch, 0:S - 1], bank(pb, S - 1, 1), vec[:, V_CW + 48 + ch:V_CW + 49 + ch],
                    uT[:, ch, 0:S - 1], ALU.mult, ALU.add).then_inc(s["conv_dve"], 1)

            def sine_argument(L, k):
                dve.wait_ge(s["filt_psum"], 2 * L + k + 1)
                a, turns, rest = (rr[:, i * S:(i + 1) * S] for i in range(3))
                c = V_FB1 + 2 * k
                ts(a, bank(7, S, rows=64), vec[0:64, c:c + 1], vec[0:64, c + 1:c + 2], ALU.add, ALU.mult)
                dve.drain()
                ts(turns, a, 1.0 / TWO_PI, ROUND, ALU.mult, ALU.add)
                dve.drain()
                ts(turns, turns, ROUND, None, ALU.subtract)
                dve.drain()
                src = a
                for part in TWO_PI_PARTS:
                    stt(rest, turns, -part, src, ALU.mult, ALU.add)
                    dve.drain()
                    src = rest
                ts(rest, rest, PI_BELOW, -PI_BELOW, ALU.min, ALU.max).then_inc(s["arg_dve"], 1)

            def rope(T, A, B, cos, sin, swap=None):
                tt(A, T, cos, ALU.mult)
                tt(B[:, :, 0], T[:, :, 1], sin, ALU.mult)
                tt(B[:, :, 1], T[:, :, 0], sin, ALU.mult)
                dve.drain()
                tt(T[:, :, 0], A[:, :, 0], B[:, :, 0], ALU.subtract)
                tt(T[:, :, 1], A[:, :, 1], B[:, :, 1], ALU.add)

            for n in ("post_dve", "xs_dve", "x_dve", "hid_dve", "o_dve"):
                dve.sem_inc(s[n], FREE)
            with dve.Fori(0, DEPTH) as L:
                dve.wait_ge(s["norm1_rms"], L + 1)
                recip(n1[:, 0:2], n1[:, 2:4])
                dve.drain()
                for t in range(SB):
                    m = ts(xn[:, t], x3[:, t], n1[:, t:t + 1], None, ALU.mult)
                m.then_inc(s["xn_ready"], 1)
                dve.wait_ge(s["vec_in"], 16 * (L + 1))
                for b in (0, 2):
                    dve.wait_ge(s["xnT_psum"], L * 4 + b + 1)
                    for i in (2 * b, 2 * b + 1):
                        m = ts(xnT[:, i], bank(b, S, (i % 2) * S), vec[:, V_N1 + i:V_N1 + i + 1], None, ALU.mult)
                    m.then_inc(s["xnT_dve"], 1)
                sine_argument(L, 0)
                dve.wait_ge(s["qkw_in"], 16 * (L + 1))
                ts(qkw[:, 0:QK], qkw[:, 0:QK], QK ** -0.5, None, ALU.mult).then_inc(s["qkw_scaled"], 1)
                dve.wait_ge(s["lat_rms"], L + 1)
                recip(lr[:, 0:4], lr[:, 4:8])
                dve.drain()
                for t in range(SB):
                    ts(lat[:, t, 0:QR], bank(3 + 2 * t, QR), lr[:, t:t + 1], None, ALU.mult)
                    copy(lat[:, t, QR:QR + ROPE], bank(3 + 2 * t, ROPE, QR))
                    m = ts(lat[:, t, QR + ROPE:LAT], bank(4 + 2 * t, KVR), lr[:, 2 + t:3 + t], None, ALU.mult)
                m.then_inc(s["lat_ready"], 1)
                dve.wait_ge(s["latT_psum"], L * 3 + 1)
                for i in (0, 1):
                    m = ts(latT[:, i], bank(2, S, i * S), vec[:, V_QA + i:V_QA + i + 1], None, ALU.mult)
                m.then_inc(s["latT_dve"], 1)
                dve.wait_ge(s["latT_psum"], L * 3 + 3)
                ts(latT[:, 4], bank(4, S), vec[:, V_KVA + 1:V_KVA + 2], None, ALU.mult).then_inc(s["latT_dve"], 1)
                conv(L, 0)
                conv(L, 1)
                sine_argument(L, 1)
                dve.wait_ge(s["consts_in"], 16)
                kraw = lat[:, :, QR:QR + ROPE]
                kr2 = small[:, 140:204].rearrange("p (b c) -> p b c", b=SB)
                krA2 = small[:, 204:268].rearrange("p (b c) -> p b c", b=SB)
                tt(krA2, kraw, kraw, ALU.mult)
                tt(kr2, kraw, qkw[:, QK + NOPE:2 * QK].unsqueeze(1).to_broadcast([P, SB, ROPE]), ALU.mult)
                dve.drain()
                reduce(kss, krA2, AX.X, ALU.add)
                dve.drain()
                cos2 = cst[:, C_COS:C_COS + SB * HALF].rearrange("p (b c) -> p b c", b=SB)
                sin2 = cst[:, C_SIN:C_SIN + SB * HALF].rearrange("p (b c) -> p b c", b=SB)
                rope(kr, krA, krB, cos2.unsqueeze(2).to_broadcast([P, SB, 2, HALF]), sin2)
                for g in range(8):
                    t, c = g // 4, g % 4
                    dve.wait_ge(s["kv_psum"], L * 8 + g + 1)
                    src = bank((3 + g % 6) % 7)
                    if c < 2:
                        m = copy(k4[:, t, 8 * c:8 * c + 8, 0:NOPE], src.rearrange("p (h c) -> p h c", h=8))
                    else:
                        m = copy(v_t[:, t, (c - 2) * 512:(c - 1) * 512], src)
                    m.then_inc(s["kv_dve"], 1)
                dve.wait_ge(s["q_act"], (L + 1) * 6)
                reduce(ssqk[:, 0:32], qsq_rows, AX.X, ALU.add)
                conv(L, 2)
                dve.wait_ge(s["ksq_act"], (L + 1) * 2)
                reduce(ssqk[:, 32:64], ksq_rows, AX.X, ALU.add)
                dve.drain()
                for t in range(SB):
                    c = slice(32 + 16 * t, 48 + 16 * t)
                    m = ts(ssqk[:, c], ssqk[:, c], kss[:, t:t + 1], None, ALU.add)
                m.then_inc(s["qkss_dve"], 1)
                conv(L, 3)
                dve.wait_ge(s["qkrms_act"], L + 1)
                recip(rqk[:, :], rqk[:, :])
                dve.drain()
                for t in range(SB):
                    conv(L, 4 + 2 * t)
                    dve.wait_ge(s["qw_pool"], L * 2 + t + 1)
                    rq = rqk[:, 16 * t:16 * t + 16]
                    rk = rqk[:, 32 + 16 * t:48 + 16 * t]
                    tt(q4[:, t], q4[:, t], rq.unsqueeze(2).to_broadcast([P, NH, QK]), ALU.mult)
                    tt(k4[:, t, :, 0:NOPE], k4[:, t, :, 0:NOPE],
                       qkw[:, QK:QK + NOPE].unsqueeze(1).to_broadcast([P, NH, NOPE]), ALU.mult)
                    dve.drain()
                    tt(k4[:, t, :, 0:NOPE], k4[:, t, :, 0:NOPE], rk.unsqueeze(2).to_broadcast([P, NH, NOPE]),
                       ALU.mult)
                    conv(L, 5 + 2 * t)
                    tt(k4[:, t, :, NOPE:QK], kr2[:, t].unsqueeze(1).to_broadcast([P, NH, ROPE]),
                       rk.unsqueeze(2).to_broadcast([P, NH, ROPE]), ALU.mult)
                    rope(q4[:, t, :, NOPE:QK].rearrange("p h (t c) -> p h t c", t=2), rpA, rpB,
                         cos2[:, t].unsqueeze(1).unsqueeze(1).to_broadcast([P, NH, 2, HALF]),
                         sin2[:, t].unsqueeze(1).to_broadcast([P, NH, HALF]))
                    dve.drain()
                nc.vector.tensor_copy(kt, kss).then_inc(s["qk_ready"], 1)
                blocks = iter(range(8, 24))
                for h in range(NH + 1):
                    g = h - 1
                    if h >= 1:
                        dve.wait_ge(s["exp_act"], L * NH + g + 1)
                        c = 2 * (g % 2)
                        recip(rsum[:, c:c + 2], rsum[:, c:c + 2])
                        dve.drain()
                        for t in range(SB):
                            m = ts(p_t[:, g % 2, t], p_t[:, g % 2, t], rsum[:, c + t:c + t + 1], None, ALU.mult)
                        m.then_inc(s["p_dve"], 1)
                    if h < NH:
                        dve.wait_ge(s["score_psum"], L * NH + h + 1)
                        reduce(nmax[:, 2 * (h % 2):2 * (h % 2) + 2],
                               bank(3 + h % 2).rearrange("p (t k) -> p t k", t=SB), AX.X, ALU.max,
                               negate=True).then_inc(s["max_dve"], 1)
                    if h >= 1:
                        dve.wait_ge(s["pT_psum"], L * NH + g + 1)
                        copy(W[:, 1024 + 512 * (g % 2):1536 + 512 * (g % 2)], bank(5 + g % 2)).then_inc(s["pT_dve"], 1)
                    if h < NH:
                        conv(L, next(blocks))
                def decayed(it):
                    if it == 0:
                        dve.wait_ge(s["decay_in"], 16 * (L + 1))
                    else:
                        dve.wait_ge(s["dft_psum"], L * 4 + it)
                        dve.wait_ge(s["habs_act"], L * 4 + it)
                    dve.wait_ge(s["f3_psum"], L * 4 + it + 1)
                    c = it % 2
                    for t in range(SB):
                        m = tt(hflt[:, t], bank(2 * (it % 2) + t), decay[:, t, c * HW:(c + 1) * HW], ALU.mult)
                    m.then_inc(s["h_dve"], 1)

                decayed(0)
                for it in range(4):
                    n, c = it // 2, it % 2
                    cs = slice(c * HW, (c + 1) * HW)
                    if it < 3:
                        decayed(it + 1)
                    dve.wait_ge(s["dft_psum"], L * 4 + it + 1)
                    for f in (2, 0, 1):
                        copy(spec[:, n, f, cs], bank(5 + f)).then_inc(s["spec_dve"], 1)
                    dve.wait_ge(s["hsum_psum"], L * 4 + it + 1)
                    k = n * DB + 4 * c
                    copy(hsum[:, k:k + 4], bank(4, 4)).then_inc(s["spec_dve"], 1)
                    dve.drain()
                    recip(hinv[:, k:k + 4], hsum[:, k:k + 4])
                    tt(hskip[:, k:k + 4], hsum[:, k:k + 4], vec[:, V_SKIP + k:V_SKIP + k + 4], ALU.mult)
                    dve.drain()

                def products(it):
                    n, c = it // 2, it % 2
                    cs = slice(c * HW, (c + 1) * HW)
                    dve.drain()
                    dve.wait_ge(s["zf_psum"], L * 4 + it + 1)
                    dve.wait_ge(s["swap_act"], L * 4 + it + 1)
                    sp_ = [spec[:, n, f, cs] for f in range(4)]
                    tt(prod[:, 0], bank(2), sp_[0], ALU.mult)
                    tt(prod[:, 2], bank(2), sp_[1], ALU.mult)
                    tt(prod[:, 1], bank(3), sp_[1], ALU.mult)
                    tt(prod[:, 3], bank(3), sp_[0], ALU.mult)
                    tt(prod2[:, 0], bank(4), sp_[2], ALU.mult)
                    tt(prod2[:, 1], bank(4), sp_[3], ALU.mult).then_inc(s["prod_dve"], 1)

                def spectrum(it):
                    dve.drain()
                    if it >= 1:
                        dve.wait_ge(s["y_psum"], L * 8 + 2 * it)
                    tt(yT_t[:, 0], prod[:, 0], prod[:, 1], ALU.subtract)
                    tt(yT_t[:, 1], prod[:, 2], prod[:, 3], ALU.add)
                    dve.wait_ge(s["shift_act"], L * 4 + it + 1)
                    tt(yT_t[0:64, 2], prod2[0:64, 0], prod2[0:64, 2], ALU.subtract)
                    tt(yT_t[64:128, 2], prod2[64:128, 1], prod2[64:128, 2], ALU.add).then_inc(s["yf_dve"], 1)

                def gate_z(it):
                    n, c = it // 2, it % 2
                    for jj in range(2):
                        dve.wait_ge(s["y_psum"], L * 8 + 2 * it + jj + 1)
                        b0 = 4 * c + 2 * jj
                        for r in range(2):
                            k = n * DB + b0 + r
                            stt(uT[:, b0 + r], uT[:, b0 + r], hskip[:, k:k + 1], bank(5 + jj, S, r * S),
                                ALU.mult, ALU.add)
                        dve.drain()
                        for r in range(2):
                            k = n * DB + b0 + r
                            m = stt(uT[:, b0 + r], uT[:, b0 + r], hinv[:, k:k + 1], uT[:, 8 * (n + 1) + b0 + r],
                                    ALU.mult, ALU.mult)
                    m.then_inc(s["post_dve"], 1)

                products(0)
                spectrum(0)
                for it in range(4):
                    if it < 3:
                        products(it + 1)
                    gate_z(it)
                    if it < 3:
                        spectrum(it + 1)
                for i in range(DB):
                    dve.wait_ge(s["sig_act"], L * 8 + i + 1)
                    dve.wait_ge(s["branch_psum"], L * 8 + i + 1)
                    gm = gm_t[:, i % 2]
                    tt(gm, sg[:, i % 2], bank(2 * (i % 2) + 1), ALU.mult)
                    dve.drain()
                    tt(mT[:, i], gm[:, 0:S], gm[:, S:2 * S], ALU.add).then_inc(s["merged_dve"], 1)
                for k in range(4):
                    c, t = k // 2, k % 2
                    dve.wait_ge(s["wout_psum"], L * 4 + k + 1)
                    xc = x3[:, t, c * 512:(c + 1) * 512]
                    m = tt(xc, xc, bank(4 + k), ALU.add)
                m.then_inc(s["xmid_dve"], 1)
                dve.wait_ge(s["norm2_rms"], L + 1)
                recip(n2[:, 0:2], n2[:, 2:4])
                dve.drain()
                for t in range(SB):
                    m = ts(xn2[:, t], x3[:, t], n2[:, t:t + 1], None, ALU.mult)
                m.then_inc(s["xn2_dve"], 1)
                dve.wait_ge(s["fvec_in"], 16 * (L + 1))
                for b in (0, 2):
                    dve.wait_ge(s["xn2T_psum"], L * 4 + b + 1)
                    for i in (2 * b, 2 * b + 1):
                        m = ts(aT[:, i], bank(b, S, (i % 2) * S), fvec[:, W_N2 + i:W_N2 + i + 1], None, ALU.mult)
                    m.then_inc(s["xn2T_dve"], 1)
                dve.wait_ge(s["lgT_psum"], L + 1)
                copy(lgT, bank(4, S, rows=E)).then_inc(s["lgT_dve"], 1)
                dve.wait_ge(s["lg_psum"], L + 1)
                reduce(lmax[:, 0:2], bank(5, SB * E).rearrange("p (t e) -> p t e", t=SB), AX.X, ALU.max,
                       negate=True).then_inc(s["lmax_dve"], 1)
                dve.wait_ge(s["lexp_act"], L + 1)
                recip(lmax[:, 2:4], lmax[:, 2:4])
                dve.drain()
                for t in range(SB):
                    m = ts(aff[:, t], aff[:, t], lmax[:, 2 + t:3 + t], None, ALU.mult)
                m.then_inc(s["aff_dve"], 1)
                dve.wait_ge(s["affT_psum"], L + 1)
                copy(work, bank(6, S, rows=E))
                dve.drain()
                for _ in range(CAP // 8):
                    nc.vector.max(top8, work)
                    dve.drain()
                    nc.vector.match_replace(work, top8, work, -1.0)
                    dve.drain()
                ts(picked, work, 0.0, None, ALU.is_lt)
                dve.drain()
                nc.vector.tensor_tensor_scan(rank, picked, picked, 0.0, ALU.add, ALU.max)
                dve.drain()
                tt(ptok, rank, picked, ALU.mult)
                dve.drain()
                ts(ptok, ptok, 1.0, None, ALU.subtract).then_inc(s["pos_dve"], 1)
                dve.wait_ge(s["pos_psum"], L + 1)
                copy(pos_flat, bank(7, SB * E))
                dve.drain()

                with dve.Fori(0, NG) as g:
                    for t in range(SB):
                        m = tt(pick[:, t].rearrange("p (q c) -> p q c", q=GROUP),
                               cst[:, C_IOTA:C_IOTA + P].rearrange("p (q c) -> p q c", q=GROUP),
                               pos[:, t, ds(g * GROUP, GROUP)].unsqueeze(2).to_broadcast([P, GROUP, CAP]),
                               ALU.is_equal)
                    m.then_inc(s["pick_dve"], 1)
                    dve.wait_ge(s["xs_psum"], L * NG + g + 1)
                    for b in range(2):
                        m = tt(xs[:, 4 * b:4 * b + 4], bank(b).rearrange("p (i c) -> p i c", i=4),
                               fvec[:, W_N2 + 4 * b:W_N2 + 4 * b + 4].unsqueeze(2).to_broadcast([P, 4, P]),
                               ALU.mult)
                    m.then_inc(s["xs_dve"], 1)
                    for q in range(GROUP):
                        e = g * GROUP + q
                        n = L * E + e
                        for t in range(SB):
                            m = ts(gsel[:, t], cst[:, C_IOTA:C_IOTA + P], pos[:, t, ds(e, 1)],
                                   aff[:, t, ds(e, 1)], ALU.is_equal, ALU.mult)
                        m.then_inc(s["gsel_dve"], 1)
                        dve.wait_ge(s["sil_act"], n + 1 + FREE)
                        dve.wait_ge(s["up_done"], n + 1 + FREE)
                        tt(hid_e, sil, bank(3, FT), ALU.mult).then_inc(s["hid_dve"], 1)
                        dve.wait_ge(s["hT_psum"], n + 1)
                        copy(hT[:, 0:2 * P], bank(5, 2 * P))
                        copy(hT[0:KF[2], 2 * P:3 * P], bank(5, P, 2 * P, rows=KF[2])).then_inc(s["hT_dve"], 1)
                        dve.wait_ge(s["o_psum"], n + 1 + FREE)
                        copy(o_sb[:, 512:1024], bank(1)).then_inc(s["o_dve"], 1)
                        for k in range(4):
                            t, c = k // 2, k % 2
                            dve.wait_ge(s["y2_psum"], n * 4 + k + 1)
                            xc = x3[:, t, c * 512:(c + 1) * 512]
                            tt(xc, xc, bank(6 + k % 2), ALU.add).then_inc(s["x_dve"], 1)


def constants():
    import numpy as np
    k = np.arange(NF // 2)[:, None]
    th = np.pi * (2 * k + 1) / NF
    f = th * np.arange(S)[None, :]
    g = th * (np.arange(S)[None, :] + S // 2)
    cf, sf, ci, si = np.cos(f), -np.sin(f), 2 / NF * np.cos(g), -2 / NF * np.sin(g)
    fwd = np.concatenate([cf[:P], sf[:P], cf[P:], sf[P:]])
    inv = np.concatenate([ci[:P], si[:P], ci[P:], si[P:]])
    c = np.zeros((P, C_N), np.float32)
    c[:, C_ID:C_ID + P] = np.eye(P)
    c[:, C_F:C_F + SB * NF] = fwd.T.reshape(SB, P, NF).transpose(1, 0, 2).reshape(P, -1)
    c[:, C_IF:C_IF + 3 * S] = inv.reshape(3, P, S).transpose(1, 0, 2).reshape(P, -1)
    f32 = np.float32
    inv_freq = f32(10000.0) ** (-np.arange(0, ROPE, 2, dtype=f32) / f32(ROPE))
    ang = (np.arange(S, dtype=f32)[:, None] * inv_freq[None]).astype(f32)
    for at, tab in ((C_COS, np.cos(ang)), (C_SIN, np.sin(ang))):
        c[:, at:at + SB * HALF] = tab.reshape(SB, P, HALF).transpose(1, 0, 2).reshape(P, -1)
    c[:, C_IOTA:C_IOTA + P] = np.arange(P)[None] % CAP
    c[:, C_ONES] = 1.0
    pos = np.arange(S, dtype=f32)
    tm = pos / f32(S)
    bands = 16
    w = f32(2.0 * np.pi) * tm[:, None] * np.linspace(1e-4, bands - 1, bands, dtype=f32)[None]
    feats = np.concatenate([tm[:, None], np.cos(w), np.sin(w)], -1)
    c[0:33, C_FEAT:C_FEAT + S] = feats.T
    c[:, C_EPS] = EPS
    tau = np.abs(pos - S // 2) / f32(S // 2)
    low, high = np.log(1e-2) / 1.5, np.log(1e-2) / 0.3
    delta = np.abs(np.linspace(low, high, D, dtype=f32))
    decay = np.exp(-tau[:, None] * delta[None]).astype(f32)
    decay = np.ascontiguousarray(decay.reshape(SB, P, D).transpose(1, 0, 2))
    return c, decay


def kernel(**inputs):
    import concourse.bacc as bacc
    import numpy as np
    from concourse.bass_utils import run_bass_kernel_spmd

    a = {k: np.asarray(v) for k, v in inputs.items()}

    def cols(v):
        return v.reshape(DEPTH, -1, P).transpose(0, 2, 1)

    def k_major(w):
        return w.reshape(DEPTH, -1, P, w.shape[-1]).transpose(0, 2, 1, 3)

    small = np.zeros((DEPTH, P, 4), np.float32)
    for i, name in enumerate(("filt_b1", "filt_freq1", "filt_b2", "filt_freq2")):
        small[:, 0:64, i] = a[name]
    vecs = np.concatenate([cols(a["norm1_w"]), cols(a["q_a_norm_w"]), cols(a["kv_a_norm_w"]),
                           cols(a["short_conv_w"].reshape(DEPTH, -1)), cols(a["short_conv_b"]),
                           cols(a["filt_skip"].reshape(DEPTH, -1)), small], 2)
    fvecs = np.concatenate([cols(a["norm2_w"]), k_major(a["router_w"]).reshape(DEPTH, P, -1)], 2)
    qkw = np.concatenate([a["q_norm_w"], a["k_norm_w"]], 1)
    w_in = k_major(a["w_in"])
    kv0, rope0, hy0 = QR, QR + KVR, QR + KVR + ROPE
    gate0 = hy0 + 3 * D
    w_lat = np.concatenate([w_in[..., 0:QR], w_in[..., rope0:hy0], w_in[..., kv0:rope0]], 3).reshape(DEPTH, P, -1)
    w_kv = k_major(a["w_kv_b"]).reshape(DEPTH, P, KVB, NH, 2, NOPE).transpose(0, 1, 2, 4, 3, 5)
    units = [w_kv.reshape(DEPTH, P, UNIT)]

    def half(w, c0):
        return w[..., c0:c0 + HW].reshape(DEPTH, P, UNIT)

    w_a, w_h, w_o = k_major(a["w_attn_branch"]), k_major(a["w_hyena_branch"]), k_major(a["w_out"])
    for c in range(2):
        units += [half(w_in, hy0 + p * D + c * HW) for p in range(3)]
    for c in range(2):
        units += [half(w_in, gate0 + c * HW), half(w_in, gate0 + D + c * HW), half(w_a, c * HW), half(w_h, c * HW)]
    units += [half(w_o, 0), half(w_o, HW)]
    filt12 = np.zeros((DEPTH, 64, 192), np.float32)
    filt12[:, 0:33, 0:64] = a["filt_w1"]
    filt12[:, :, 64:128] = a["filt_w2"]
    consts, decay = constants()
    feed = {
        "x_in": a["x"], "vecs": vecs, "fvecs": fvecs, "qkw": qkw, "consts": consts, "decay": decay,
        "w_lat": w_lat, "w_q_b": a["w_q_b"], "units": np.stack(units, 1), "filt12": filt12,
        "filt3": a["filt_w3"],
        "w_gate": a["expert_w_gate"].reshape(DEPTH * E, D, FF), "w_up": a["expert_w_up"].reshape(DEPTH * E, D, FF),
        "w_down": a["expert_w_down"].reshape(DEPTH * E, FF, D),
    }
    nc = bacc.Bacc("TRN2", target_bir_lowering=False, num_devices=1)
    arrays, args = {}, []
    for name, v in feed.items():
        v = np.ascontiguousarray(v)
        arrays[name + "_dram"] = v
        args.append(nc.dram_tensor(name + "_dram", v.shape, mybir.dt.from_np(v.dtype), kind="ExternalInput").ap())
    args.append(nc.dram_tensor("out_dram", (1, S, D), F32, kind="ExternalOutput").ap())
    build(nc, *args)
    r = run_bass_kernel_spmd(nc, [arrays], core_ids=[0])
    return r.results[0]["out_dram"]
```

```python
from contextlib import ExitStack

import concourse.bass as bass
from concourse import mybir

F32 = mybir.dt.float32
ALU = mybir.AluOpType
ACT = mybir.ActivationFunctionType
AX = mybir.AxisListType
ds = bass.ds

P = 128
D, S, DEPTH = 1024, 256, 2
SB, DB = S // P, D // P
NH, NOPE, ROPE, VD = 16, 64, 32, 64
QK = NOPE + ROPE
HALF = ROPE // 2
QR, KVR = 384, 256
LAT = QR + ROPE + KVR
QB, KVB = QR // P, KVR // P
E, FF = 16, 1408
CAP = 2 * S // E
GROUP = P // CAP
NG = E // GROUP
CT = P // CAP
FT = FF // CT
KF = [P, P, FT - 2 * P]
NF = 384
HW = 512
EPS = 1e-6

FREE = 1
X_FREE = 3

UNIT = DB * 512
NU, RING = 17, 5
UNIT0 = 2048
SLOT = DB * FF
M2AT = DB * LAT


def unit_slot(n):
    return (n + 2) % RING


def uT_block(b):
    return b // 4 % 3 * DB + b // 12 * 4 + b % 4


UNITS_IN_SLOT = [sum(unit_slot(n) == s for n in range(NU)) for s in range(RING)]

C_ID, C_F, C_IF = 0, 128, 128 + SB * NF
C_COS = C_IF + 3 * S
C_SIN = C_COS + SB * HALF
C_IOTA = C_SIN + SB * HALF
C_ONES = C_IOTA + P
C_FEAT = C_ONES + 1
C_EPS = C_FEAT + S
C_N = C_EPS + 1
KSC = QR + KVR
TWO_PI = 6.283185307179586
TWO_PI_PARTS = (6.28125, 0.0019350051879882812, 3.0199159795074593e-07)
ROUND = 12582912.0
PI_BELOW = 3.1415925
V_N1, V_QA, V_KVA = 0, DB, DB + QB
V_CW = V_KVA + KVB
V_CB = V_CW + 3 * 24
V_SKIP = V_CB + 24
V_FB1 = V_SKIP + 16
V_N = V_FB1 + 4
W_N2, W_RT = 0, DB
W_N = DB + DB * E


def build(nc, x_in, vecs, fvecs, qkw_in, consts_in, decay_in, w_lat, w_q_b, units_in,
          filt12, filt3, w_gate, w_up, w_down, out):
    with ExitStack() as ctx:
        def sb(name, cols):
            return ctx.enter_context(nc.sbuf_tensor(name, [P, cols], F32))

        def sem(name):
            return ctx.enter_context(nc.semaphore(name))

        ring = sb("ring", 2 * SLOT)
        R = sb("region", 12 * 1024)
        xt = sb("x", SB * D)
        xnT_t = sb("xnT", DB * S)
        uT_t = sb("uT", 24 * S)
        aT_t = sb("attnT", DB * S)
        W = sb("work", 3072)
        cst = sb("consts", C_N)
        vec = sb("vec", V_N)
        fvec = sb("fvec", W_N)
        qkw = sb("qkw", 2 * QK)
        small = sb("small", 340)
        ps_t = ctx.enter_context(nc.psum_tensor("ps", [P, 8, 512], F32))

        def bank(b, n=512, off=0, rows=P, row0=0):
            return ps_t[row0:row0 + rows, b, off:off + n]

        ident = cst[:, C_ID:C_ID + P]
        x3 = xt[:, :].rearrange("p (b d) -> p b d", b=SB)
        xnT = xnT_t[:, :].rearrange("p (i s) -> p i s", i=DB)
        xn2 = xnT_t[:, :].rearrange("p (b d) -> p b d", b=SB)
        uT = uT_t[:, :].rearrange("p (c s) -> p c s", s=S)
        aT = aT_t[:, :].rearrange("p (i s) -> p i s", s=S)
        xn = R[:, 0:SB * D].rearrange("p (b d) -> p b d", b=SB)
        q_t = R[:, 0:SB * NH * QK].rearrange("p (b c) -> p b c", b=SB)
        q4 = R[:, 0:SB * NH * QK].rearrange("p (b h c) -> p b h c", b=SB, h=NH)
        k0 = SB * NH * QK
        k4 = R[:, k0:2 * k0].rearrange("p (b h c) -> p b h c", b=SB, h=NH)
        v_t = R[:, 2 * k0:2 * k0 + SB * D].rearrange("p (b c) -> p b c", b=SB)
        w3 = R[0:64, 8192:8192 + 2048]
        w12 = R[0:64, 10240:10432]
        h2T = R[0:64, 10432:10432 + S]
        h1T = R[0:64, 10688:10688 + S]
        rr = R[0:64, 10944:10944 + 768]
        habs = R[:, 10688:11712]
        spec = R[:, 0:8192].rearrange("p (n b c) -> p n b c", n=2, b=4)
        z_t = R[:, 8192:10240].rearrange("p (h b c) -> p h b c", h=2, b=SB)
        prod = R[:, 10240:12288].rearrange("p (k c) -> p k c", k=4)
        lat = W[:, 0:SB * LAT].rearrange("p (b c) -> p b c", b=SB)
        latT = W[:, SB * LAT:SB * LAT + 5 * S].rearrange("p (i s) -> p i s", s=S)
        p_t = W[:, 0:1024].rearrange("p (t b k) -> p t b k", t=2, b=SB)
        pT_t = W[:, 1024:2048].rearrange("p (t b k) -> p t b k", t=2, b=SB)
        qkT = W[:, 2048:3072].rearrange("p (t c) -> p t c", t=2)
        decay = W[:, 0:2048].rearrange("p (b c) -> p b c", b=SB)
        hflt = W[:, 2048:3072].rearrange("p (b c) -> p b c", b=SB)
        yT_t = W[:, 0:1536].rearrange("p (b c) -> p b c", b=3)
        prod2 = W[:, 1536:3072].rearrange("p (b c) -> p b c", b=3)
        sg = W[:, 0:1024].rearrange("p (t c) -> p t c", t=2)
        gm_t = W[:, 1024:2048].rearrange("p (t c) -> p t c", t=2)
        qsq = uT_t[:, 3072:6144].rearrange("p (b h c) -> p b h c", b=SB, h=NH)
        ksq = aT_t[:, :].rearrange("p (b h c) -> p b h c", b=SB, h=NH)
        rpA = uT_t[:, 3072:3584].rearrange("p (h t c) -> p h t c", h=NH, t=2)
        rpB = uT_t[:, 3584:4096].rearrange("p (h t c) -> p h t c", h=NH, t=2)
        mT = uT_t[:, 2048:4096].rearrange("p (i s) -> p i s", s=S)
        xs = uT_t[:, 0:1024].rearrange("p (i c) -> p i c", i=DB)
        o_sb = uT_t[:, 1024:2048]
        pick = uT_t[:, 2048:2304].rearrange("p (b c) -> p b c", b=SB)
        gsel = uT_t[:, 2304:2560].rearrange("p (b c) -> p b c", b=SB)
        gselT = uT_t[:, 2560:2816]
        sil = uT_t[:, 2816:2816 + FT]
        hid_e = uT_t[:, 3200:3200 + FT]
        hT = uT_t[:, 3584:3584 + 3 * P]
        lgT = uT_t[0:E, 4096:4096 + S]
        work = uT_t[0:E, 4352:4352 + S]
        rank = uT_t[0:E, 4608:4608 + S]
        picked = uT_t[0:E, 4864:4864 + S]
        ptok = uT_t[0:E, 5120:5120 + S]
        top8 = uT_t[0:E, 5376:5384]
        aff = uT_t[:, 5400:5400 + SB * E].rearrange("p (b e) -> p b e", b=SB)
        pos = uT_t[:, 5440:5440 + SB * E].rearrange("p (b e) -> p b e", b=SB)
        ones = cst[:, C_ONES:C_ONES + 1]

        n1 = small[:, 0:4]
        lr = small[:, 4:12]
        ssqk = small[:, 12:76]
        rqk = small[:, 76:140]
        kr = small[:, 140:204].rearrange("p (b t c) -> p b t c", b=SB, t=2)
        krA = small[:, 204:268].rearrange("p (b t c) -> p b t c", b=SB, t=2)
        kss = small[:, 268:270]
        nmax = small[:, 270:274]
        rsum = small[:, 274:278]
        n2 = small[:, 278:282]
        lmax = small[:, 282:286]
        kt = small[:, 286:288]
        n2b = small[:, 336:338]
        hsum, hinv, hskip = small[:, 288:304], small[:, 304:320], small[:, 320:336]
        krB = uT_t[:, 2600:2664].rearrange("p (b t c) -> p b t c", b=SB, t=2)
        qsq_rows = uT_t[:, 3072:6144].rearrange("p (r c) -> p r c", c=QK)
        ksq_rows = aT_t[:, :].rearrange("p (r c) -> p r c", c=NOPE)
        pos_flat = uT_t[:, 5440:5440 + SB * E]

        sg_early = ring[:, 0:UNIT0].rearrange("p (i c) -> p i c", i=4)
        m1 = ring[:, 0:M2AT].rearrange("p (i c) -> p i c", i=DB)
        m2 = ring[:, M2AT:M2AT + QB * NH * QK].rearrange("p (i c) -> p i c", i=QB)

        def unit(n):
            a = UNIT0 + unit_slot(n) * UNIT
            return ring[:, a:a + UNIT]

        def unit8(n):
            return unit(n).rearrange("p (i c) -> p i c", i=DB)

        wkv = unit(0).rearrange("p (i c) -> p i c", i=KVB)
        wg = ring[:, 0:SLOT].rearrange("p (i f) -> p i f", i=DB)
        wu = ring[:, SLOT:2 * SLOT].rearrange("p (i f) -> p i f", i=DB)
        wd = R[:, :].rearrange("p (j b d) -> p j b d", j=CT, b=3)

        names = """one_dve x_in consts_in vec_in fvec_in qkw_in filt_in decay_in wqb_in wg_in wu_in out_done
        norm1_rms xn_ready xnT_psum xnT_dve xnT_act lat_psum lat_rms lat_ready latT_psum latT_dve latT_act
        filt_psum arg_dve sin_act q_psum q_act kv_psum kv_dve ksq_act qkss_dve qkrms_act qw_pool kw_pool rqk_dve qkr_pool qkw_scaled qk_ready
        proj_psum conv_act conv_dve
        qkT_psum qkT_act score_psum max_dve exp_act p_dve pT_psum pT_dve pv_psum oT_act
        f3_psum h_dve habs_act habs_pool dft_psum hsum_psum spec_dve swap_act
        zT_psum z_act zf_psum prod_dve shift_act yf_dve y_psum post_dve
        gate_psum branch_psum sig_act merged_dve
        wout_psum xmid_dve norm2_rms xn2_act xn2T_psum xn2T_dve xn2T_act lgT_psum lgT_dve lg_psum lmax_dve lexp_act
        aff_dve affT_psum pos_dve pos_psum
        pick_dve xs_psum xs_dve gsel_dve gselT_psum gselT_act gate_half gate_done up_done sil_act hid_dve hT_psum hT_dve
        o_psum o_act o_dve y2_psum x_dve""".split()
        s = {n: sem(n) for n in names}
        wlat_in = [sem(f"wlat_in{k}") for k in range(2)]
        wd_in = [sem(f"wd_in{b}") for b in range(3)]
        unit_in = [sem(f"unit_in{i}") for i in range(RING)]
        block = ctx.enter_context(nc.Block())

        @block.sync
        def _(sp):
            sp.dma_start(x3, x_in.rearrange("a (b p) d -> p (a b) d", p=P)).then_inc(s["x_in"], 16)
            sp.dma_start(cst[:, :], consts_in).then_inc(s["consts_in"], 16)
            with sp.Fori(0, DEPTH) as L:
                def unit_is_used(n):
                    if n == 0:
                        sp.wait_ge(s["kv_psum"], (L + 1) * 8)
                    elif n < 7:
                        sp.wait_ge(s["proj_psum"], L * 24 + 4 * n)
                    elif n < 15 and (n - 7) % 4 < 2:
                        sp.wait_ge(s["gate_psum"], L * 8 + (4 if n < 11 else 8))
                    elif n < 15:
                        sp.wait_ge(s["branch_psum"], L * 8 + (4 if n < 11 else 8))
                    else:
                        sp.wait_ge(s["wout_psum"], L * 4 + 2 * (n - 14))

                sp.wait_ge(s["post_dve"], L * 4 + FREE)
                sp.dma_start(vec[:, :], vecs[L]).then_inc(s["vec_in"], 16)
                sp.dma_start(qkw[:, :], qkw_in[ds(L, 1), :].to_broadcast([P, 2 * QK])).then_inc(s["qkw_in"], 16)
                sp.wait_ge(s["gate_done"], L * E + FREE)
                for k in range(2):
                    cols = slice(M2AT // 2 * k, M2AT // 2 * (k + 1))
                    sp.dma_start(ring[:, cols], w_lat[L, :, cols]).then_inc(wlat_in[k], 16)
                sp.wait_ge(s["up_done"], L * E + FREE)
                sp.dma_start(unit(1), units_in[L, 1]).then_inc(unit_in[unit_slot(1)], 16)
                sp.dma_start(m2, w_q_b[L].rearrange("(i p) c -> p i c", p=P)).then_inc(s["wqb_in"], 16)
                sp.dma_start(unit(0), units_in[L, 0]).then_inc(unit_in[unit_slot(0)], 16)
                sp.wait_ge(s["xs_dve"], L * NG + FREE)
                sp.dma_start(fvec[:, :], fvecs[L]).then_inc(s["fvec_in"], 16)

                def load_gate(e, half):
                    i = slice(DB // 2 * half, DB // 2 * (half + 1))
                    w = w_gate[L * E + e].rearrange("(i p) f -> p i f", p=P)
                    sp.dma_start(wg[:, i], w[:, i]).then_inc(s["wg_in"], 16)

                def load_up(e):
                    sp.dma_start(wu, w_up[L * E + e].rearrange("(i p) f -> p i f", p=P)).then_inc(s["wu_in"], 16)

                def load_down(e):
                    w = w_down[L * E + e].rearrange("(j f) d -> f j d", j=CT)
                    for b in range(3):
                        sp.dma_start(wd[0:KF[b], :, b, :], w[b * P:b * P + KF[b]]).then_inc(wd_in[b], 16)

                for n in range(2, NU):
                    if n == 3:
                        sp.wait_ge(s["q_psum"], (L + 1) * 6)
                    if n == NU - 1:
                        sp.wait_ge(s["post_dve"], (L + 1) * 4 + FREE)
                        load_down(0)
                    if n >= RING:
                        unit_is_used(n - RING)
                    sp.dma_start(unit(n), units_in[L, n]).then_inc(unit_in[unit_slot(n)], 16)

                unit_is_used(15)
                load_gate(0, 0)
                load_gate(0, 1)
                unit_is_used(16)
                load_up(0)
                with sp.Fori(1, E) as e:
                    sp.wait_ge(s["gate_half"], L * E + e)
                    load_gate(e, 0)
                    sp.wait_ge(s["gate_done"], L * E + e + FREE)
                    load_gate(e, 1)
                    sp.wait_ge(s["up_done"], L * E + e + FREE)
                    load_up(e)
                    sp.wait_ge(s["o_psum"], L * E + e + FREE)
                    load_down(e)
            sp.wait_ge(s["x_dve"], DEPTH * E * 4 + X_FREE)
            sp.dma_start(out.rearrange("a (b p) d -> p (a b) d", p=P), x3).then_inc(s["out_done"], 16)
            sp.wait_ge(s["out_done"], 16)

        @block.gpsimd
        def _(pool):
            with pool.Fori(0, DEPTH) as L:
                pool.wait_ge(s["qkw_scaled"], L + 1)
                for b in range(SB):
                    pool.wait_ge(s["q_act"], L * 6 + 3 * (b + 1))
                    nc.gpsimd.tensor_tensor(
                        q4[:, b], q4[:, b], qkw[:, 0:QK].unsqueeze(1).to_broadcast([P, NH, QK]),
                        ALU.mult).then_inc(s["qw_pool"], 1)
                for b in range(SB):
                    pool.wait_ge(s["ksq_act"], L * 2 + b + 1)
                    nc.gpsimd.tensor_tensor(
                        k4[:, b, :, 0:NOPE], k4[:, b, :, 0:NOPE],
                        qkw[:, QK:QK + NOPE].unsqueeze(1).to_broadcast([P, NH, NOPE]),
                        ALU.mult).then_inc(s["kw_pool"], 1)
                pool.drain()
                pool.wait_ge(s["rqk_dve"], L + 1)
                nc.gpsimd.tensor_tensor(
                    q4[:, 1], q4[:, 1], rqk[:, NH:2 * NH].unsqueeze(2).to_broadcast([P, NH, QK]),
                    ALU.mult).then_inc(s["qkr_pool"], 1)
                nc.gpsimd.tensor_tensor(
                    k4[:, 1, :, 0:NOPE], k4[:, 1, :, 0:NOPE],
                    rqk[:, 3 * NH:4 * NH].unsqueeze(2).to_broadcast([P, NH, NOPE]),
                    ALU.mult).then_inc(s["qkr_pool"], 1)
                for it in range(4):
                    pool.wait_ge(s["habs_act"], L * 4 + it + 1)
                    nc.gpsimd.tensor_tensor(habs[:, 0:HW], habs[:, 0:HW], habs[:, HW:2 * HW],
                                            ALU.add).then_inc(s["habs_pool"], 1)

        @block.tensor
        def _(pe):
            mm = nc.tensor.matmul
            tp = nc.tensor.transpose

            for n in ("gate_done", "up_done", "o_psum"):
                pe.sem_inc(s[n], FREE)
            with pe.Fori(0, DEPTH) as L:
                pe.wait_ge(s["consts_in"], 16)
                pe.wait_ge(s["xn_ready"], L + 1)
                for b in range(4):
                    for c in range(4):
                        i, t = 2 * b + c // 2, c % 2
                        m = tp(bank(b, P, c * P), xn[:, t, i * P:(i + 1) * P], ident)
                    m.then_inc(s["xnT_psum"], 1)
                pe.wait_ge(s["xnT_dve"], 2 * (L + 1))
                pe.wait_ge(s["xnT_act"], 2 * (L + 1))
                for t in range(SB):
                    for i in range(DB):
                        if t == 0 and i % 4 == 0:
                            pe.wait_ge(wlat_in[i // 4], 16 * (L + 1))
                        mm(bank(3 + 2 * t, QR + ROPE), xnT[:, i, t * P:(t + 1) * P], m1[:, i, 0:QR + ROPE],
                           start=i == 0, stop=i == DB - 1)
                    for i in range(DB):
                        m = mm(bank(4 + 2 * t, KVR), xnT[:, i, t * P:(t + 1) * P], m1[:, i, QR + ROPE:LAT],
                               start=i == 0, stop=i == DB - 1)
                m.then_inc(s["lat_psum"], 1)
                blocks = iter(range(24))

                def next_block():
                    b = next(blocks)
                    n, j = 1 + b // 4, b % 4
                    if j == 0:
                        pe.wait_ge(unit_in[unit_slot(n)],
                                   16 * (L * UNITS_IN_SLOT[unit_slot(n)] + n // RING + 1))
                    if b >= 2:
                        pe.wait_ge(s["conv_dve"], L * 24 + b - 1)
                    half_block(b, 0)

                    def rest():
                        half_block(b, 1).then_inc(s["proj_psum"], 1)
                    return rest

                def half_block(b, k):
                    n, j = 1 + b // 4, b % 4
                    for i in range(4 * k, 4 * k + 4):
                        m = mm(bank(b % 2, S), unit8(n)[:, i, j * P:(j + 1) * P], xnT[:, i],
                               start=i == 0, stop=i == DB - 1)
                    return m

                next_block()()
                next_block()()
                pe.wait_ge(s["lat_ready"], L + 1)
                for i in range(5):
                    c0 = i * P if i < QB else QR + ROPE + (i - QB) * P
                    for t in range(SB):
                        m = tp(bank(2 + i // 2, P, (i % 2) * S + t * P), lat[:, t, c0:c0 + P], ident)
                    if i % 2 or i == 4:
                        m.then_inc(s["latT_psum"], 1)
                pe.wait_ge(s["consts_in"], 16)
                pe.wait_ge(s["filt_in"], 32 * (L + 1))
                mm(bank(7, S), w12[0:33, 0:P], cst[0:33, C_FEAT:C_FEAT + S],
                   start=True, stop=True).then_inc(s["filt_psum"], 1)
                pe.wait_ge(s["wqb_in"], 16 * (L + 1))
                pe.wait_ge(s["latT_dve"], 2 * (L + 1))
                pe.wait_ge(s["latT_act"], L + 1)
                for g in range(6):
                    t, c = g // 3, g % 3
                    if g >= 4:
                        pe.wait_ge(s["conv_dve"], L * 24 + g - 3)
                    for i in range(QB):
                        m = mm(bank((3 + g) % 7), latT[:, i, t * P:(t + 1) * P], m2[:, i, c * 512:(c + 1) * 512],
                               start=i == 0, stop=i == QB - 1)
                    m.then_inc(s["q_psum"], 1)
                    if g == 1:
                        pe.wait_ge(s["consts_in"], 16)
                        pe.wait_ge(s["sin_act"], 2 * L + 1)
                        mm(bank(7, S), w12[:, 64:64 + P], h1T, start=True, stop=True).then_inc(s["filt_psum"], 1)
                pe.wait_ge(unit_in[unit_slot(0)], 16 * (L * UNITS_IN_SLOT[unit_slot(0)] + 1))
                for g in range(8):
                    t, c = g // 4, g % 4
                    if g < 6:
                        pe.wait_ge(s["q_act"], L * 6 + g + 1)
                    else:
                        pe.wait_ge(s["kv_dve"], L * 8 + g - 5)
                    for i in range(KVB):
                        m = mm(bank((3 + g % 6) % 7), latT[:, QB + i, t * P:(t + 1) * P], wkv[:, i, c * 512:(c + 1) * 512],
                               start=i == 0, stop=i == KVB - 1)
                    m.then_inc(s["kv_psum"], 1)
                pe.wait_ge(s["kv_dve"], (L + 1) * 8)

                gates = iter([(i, g) for i in range(4) for g in range(2)])

                def next_gates():
                    i, g = next(gates)
                    if i == 0:
                        n = 7 + g
                        pe.wait_ge(unit_in[unit_slot(n)], 16 * (L * UNITS_IN_SLOT[unit_slot(n)] + n // RING + 1))
                    elif i >= 2 and g == 0:
                        pe.wait_ge(s["sig_act"], L * 8 + i)
                    gate_product(i, g, bank(7 if i else 2, S, g * S))

                def gate_product(i, g, dst):
                    for k in range(DB):
                        m = mm(dst, unit8(7 + 4 * (i // 4) + g)[:, k, i % 4 * P:(i % 4 + 1) * P], xnT[:, k],
                               start=k == 0, stop=k == DB - 1)
                    if g == 1:
                        m.then_inc(s["gate_psum"], 1)

                for _ in range(6):
                    next_block()()
                pe.wait_ge(s["qk_ready"], L + 1)
                pe.wait_ge(s["qkr_pool"], (L + 1) * 2)
                for h in range(NH + 1):
                    if h < NH:
                        if h >= 1:
                            pe.wait_ge(s["qkT_act"], L * NH + h)
                        for w, src in enumerate((q4, k4)):
                            for t in range(SB):
                                m = tp(bank(2, P, w * S + t * P, rows=QK), src[:, t, h], ident)
                        m.then_inc(s["qkT_psum"], 1)
                        rest_of_block = next_block()
                        pe.wait_ge(s["qkT_act"], L * NH + h + 1)
                        if h >= 2:
                            pe.wait_ge(s["exp_act"], L * NH + h - 1)
                        for t in range(SB):
                            m = mm(bank(3 + h % 2, S, t * S), qkT[0:QK, h % 2, t * P:(t + 1) * P],
                                   qkT[0:QK, h % 2, S:2 * S], start=True, stop=True)
                        m.then_inc(s["score_psum"], 1)
                    if h >= 1:
                        g = h - 1
                        pe.wait_ge(s["p_dve"], L * NH + g + 1)
                        if g >= 2:
                            pe.wait_ge(s["pT_dve"], L * NH + g - 1)
                        for kb in range(SB):
                            for t in range(SB):
                                m = tp(bank(5 + g % 2, P, kb * S + t * P), p_t[:, g % 2, t, kb * P:(kb + 1) * P], ident)
                        m.then_inc(s["pT_psum"], 1)
                    if h < NH:
                        rest_of_block()
                    else:
                        next_gates()
                    if h >= 1:
                        pe.wait_ge(s["pT_dve"], L * NH + g + 1)
                        if g % 2 == 0 and g >= 2:
                            pe.wait_ge(s["oT_act"], L * (NH // 2) + g // 2)
                        for kb in range(SB):
                            m = mm(bank(7, S, rows=VD, row0=VD * (g % 2)), v_t[:, kb, g * VD:(g + 1) * VD],
                                   pT_t[:, g % 2, kb], start=kb == 0, stop=kb == SB - 1)
                        m.then_inc(s["pv_psum"], 1)
                next_gates()
                pe.wait_ge(s["conv_dve"], (L + 1) * 24)
                pe.wait_ge(s["oT_act"], (L + 1) * (NH // 2))

                def filter_time(it):
                    n, c = it // 2, it % 2
                    if it == 0:
                        pe.wait_ge(s["sin_act"], 2 * L + 2)
                    if it == 1:
                        pe.wait_ge(s["sig_act"], L * 8 + 1)
                    if it >= 2:
                        pe.wait_ge(s["h_dve"], L * 4 + it - 1)
                    for t in range(SB):
                        m = mm(bank(2 * (it % 2) + t), h2T[:, t * P:(t + 1) * P],
                               w3[:, n * D + c * HW:n * D + (c + 1) * HW], start=True, stop=True)
                    m.then_inc(s["f3_psum"], 1)

                def z_transposed(it):
                    n, c = it // 2, it % 2
                    if it >= 2:
                        pe.wait_ge(s["post_dve"], L * 4 + it - 1 + FREE)
                    if it >= 1:
                        pe.wait_ge(s["z_act"], L * 4 + it)
                    for t in range(SB):
                        for j in range(4):
                            m = tp(bank(t, P, j * P), uT[:, 4 * c + j, t * P:(t + 1) * P], ident)
                    m.then_inc(s["zT_psum"], 1)

                filter_time(0)
                for it in range(4):
                    if it < 3:
                        filter_time(it + 1)
                    pe.wait_ge(s["h_dve"], L * 4 + it + 1)
                    if it >= 1:
                        banks_read = L * 16 + 4 * (it - 1)
                    for k, f in enumerate((2, 0, 1)):
                        if it >= 1:
                            pe.wait_ge(s["spec_dve"], banks_read + k + 1)
                        for t in range(SB):
                            m = mm(bank(5 + f), cst[:, C_F + t * NF + f * P:C_F + t * NF + (f + 1) * P],
                                   hflt[:, t], start=t == 0, stop=t == SB - 1)
                        m.then_inc(s["dft_psum"], 1)
                    if it == 3:
                        z_transposed(0)
                    pe.wait_ge(s["habs_pool"], L * 4 + it + 1)
                    if it >= 1:
                        pe.wait_ge(s["spec_dve"], banks_read + 4)
                    for j in range(4):
                        m = mm(bank(4, 1, j), habs[:, j * P:(j + 1) * P], ones, start=True, stop=True)
                    m.then_inc(s["hsum_psum"], 1)
                def to_spectrum(it):
                    if it >= 1:
                        z_transposed(it)
                    n, c = it // 2, it % 2
                    if it >= 1:
                        next_gates()
                    pe.wait_ge(s["z_act"], L * 4 + it + 1)
                    if it >= 1:
                        pe.wait_ge(s["prod_dve"], L * 4 + it)
                    for f in range(3):
                        if it == 0 and f == 2:
                            pe.wait_ge(s["spec_dve"], (L + 1) * 16)
                        for t in range(SB):
                            m = mm(bank(2 + f), cst[:, C_F + t * NF + f * P:C_F + t * NF + (f + 1) * P],
                                   z_t[:, c, t], start=t == 0, stop=t == SB - 1)
                        m.then_inc(s["zf_psum"], 1)

                def from_spectrum(it):
                    pe.wait_ge(s["yf_dve"], L * 4 + it + 1)
                    if it >= 1:
                        pe.wait_ge(s["post_dve"], L * 4 + it + FREE)
                    for j in range(4):
                        for f in range(3):
                            m = mm(bank(5 + j // 2, S, (j % 2) * S), yT_t[:, f, j * P:(j + 1) * P],
                                   cst[:, C_IF + f * S:C_IF + (f + 1) * S], start=f == 0, stop=f == 2)
                        if j % 2:
                            m.then_inc(s["y_psum"], 1)

                to_spectrum(0)
                for it in range(4):
                    if it < 3:
                        to_spectrum(it + 1)
                    from_spectrum(it)
                    if it < 3:
                        next_gates()

                for i in range(DB):
                    c, j = i // 4, i % 4
                    for g in range(0 if i >= 4 else 2, 4):
                        n = 7 + 4 * c + g
                        if j == 0:
                            pe.wait_ge(unit_in[unit_slot(n)],
                                       16 * (L * UNITS_IN_SLOT[unit_slot(n)] + n // RING + 1))
                        if g == 0 and i >= 6:
                            pe.wait_ge(s["sig_act"], L * 8 + i - 1)
                        if g == 2 and i >= 2:
                            pe.wait_ge(s["merged_dve"], L * 8 + i - 1)
                        if g == 3 and i == 0:
                            pe.wait_ge(s["post_dve"], (L + 1) * 4 + FREE)
                        dst = bank(2 * (i % 2) + g // 2, S, (g % 2) * S)
                        if g < 2:
                            gate_product(i, g, dst)
                            continue
                        for k in range(DB):
                            m = mm(dst, unit8(n)[:, k, j * P:(j + 1) * P], (aT if g == 2 else uT)[:, k],
                                   start=k == 0, stop=k == DB - 1)
                    m.then_inc(s["branch_psum"], 1)

                def x_transposed(c):
                    for t in range(SB):
                        pe.wait_ge(s["xmid_dve"], L * 4 + 2 * c + t + 1)
                        for b in (2 * c, 2 * c + 1):
                            for i in (2 * b, 2 * b + 1):
                                m = tp(bank(b, P, i % 2 * S + t * P), x3[:, t, i * P:(i + 1) * P], ident)
                            if t == 1:
                                m.then_inc(s["xn2T_psum"], 1)

                pe.wait_ge(s["merged_dve"], L * 8 + 7)
                for c in range(2):
                    n = 15 + c
                    pe.wait_ge(unit_in[unit_slot(n)], 16 * (L * UNITS_IN_SLOT[unit_slot(n)] + n // RING + 1))
                    for t in range(SB):
                        if c and t:
                            x_transposed(0)
                        for k in range(DB):
                            if c == 0 and t == 0 and k == DB - 1:
                                pe.wait_ge(s["merged_dve"], (L + 1) * 8)
                            m = mm(bank(4 + 2 * c + t), mT[:, k, t * P:(t + 1) * P], unit8(n)[:, k],
                                   start=k == 0, stop=k == DB - 1)
                        m.then_inc(s["wout_psum"], 1)
                x_transposed(1)
                pe.wait_ge(s["fvec_in"], 16 * (L + 1))
                for i in range(DB):
                    if i % 4 == 0:
                        pe.wait_ge(s["xn2T_dve"], 2 * L + 1 + i // 4)
                        pe.wait_ge(s["xn2T_act"], 2 * L + 1 + i // 4)
                    m = mm(bank(4, S, rows=E), fvec[:, W_RT + i * E:W_RT + (i + 1) * E], aT[:, i],
                           start=i == 0, stop=i == DB - 1)
                m.then_inc(s["lgT_psum"], 1)
                pe.wait_ge(s["consts_in"], 16)
                pe.wait_ge(s["lgT_dve"], L + 1)
                for t in range(SB):
                    m = tp(bank(5, E, t * E), lgT[:, t * P:(t + 1) * P], ident[0:E, 0:E])
                m.then_inc(s["lg_psum"], 1)
                pe.wait_ge(s["aff_dve"], L + 1)
                for t in range(SB):
                    m = tp(bank(6, P, t * P, rows=E), aff[:, t], ident)
                m.then_inc(s["affT_psum"], 1)
                pe.wait_ge(s["consts_in"], 16)
                pe.wait_ge(s["pos_dve"], L + 1)
                for t in range(SB):
                    m = tp(bank(7, E, t * E), ptok[:, t * P:(t + 1) * P], ident[0:E, 0:E])
                m.then_inc(s["pos_psum"], 1)

                with pe.Fori(0, NG) as g:
                    pe.wait_ge(s["pick_dve"], L * NG + g + 1)
                    pe.wait_ge(s["xn2_act"], L + 1)
                    pe.wait_ge(s["o_act"], L * E + g * GROUP + FREE)
                    pe.wait_ge(s["o_dve"], L * E + g * GROUP + FREE)
                    for i in range(DB):
                        for t in range(SB):
                            m = mm(bank(i // 4, P, (i % 4) * P), xn2[:, t, i * P:(i + 1) * P], pick[:, t],
                                   start=t == 0, stop=t == SB - 1)
                        if i % 4 == 3:
                            m.then_inc(s["xs_psum"], 1)
                    pe.wait_ge(s["xs_dve"], L * NG + g + 1 + FREE)
                    for q in range(GROUP):
                        n = L * E + g * GROUP + q
                        for w, b, arrived, read, done in ((wg, 2, "wg_in", "sil_act", "gate_done"),
                                                          (wu, 3, "wu_in", "hid_dve", "up_done")):
                            pe.wait_ge(s[arrived], (32 if w is wg else 16) * (n + 1))
                            pe.wait_ge(s[read], n + FREE)
                            for i in range(DB):
                                for j in range(CT):
                                    m = mm(bank(b, FT, rows=CAP, row0=CAP * j), xs[:, i, q * CAP:(q + 1) * CAP],
                                           w[:, i, j * FT:(j + 1) * FT], start=i == 0, stop=i == DB - 1)
                                if w is wg and i == DB // 2 - 1:
                                    m.then_inc(s["gate_half"], 1)
                            m.then_inc(s[done], 1)
                        pe.wait_ge(s["gsel_dve"], n + 1)
                        for t in range(SB):
                            m = tp(bank(4, P, t * P), gsel[:, t], ident)
                        m.then_inc(s["gselT_psum"], 1)
                        pe.wait_ge(s["hid_dve"], n + 1 + FREE)
                        for b in range(3):
                            m = tp(bank(5, P, b * P, rows=KF[b]), hid_e[:, b * P:b * P + KF[b]], ident)
                        m.then_inc(s["hT_psum"], 1)
                        pe.wait_ge(s["hT_dve"], n + 1)
                        pe.wait_ge(s["o_act"], n + FREE)
                        pe.wait_ge(s["o_dve"], n + FREE)
                        for b in range(3):
                            pe.wait_ge(wd_in[b], 16 * n + 16)
                            for c in range(2):
                                for j in range(CT):
                                    m = mm(bank(c, rows=CAP, row0=CAP * j),
                                           hT[0:KF[b], b * P + CAP * j:b * P + CAP * (j + 1)],
                                           wd[0:KF[b], j, b, c * 512:(c + 1) * 512], start=b == 0, stop=b == 2)
                        m.then_inc(s["o_psum"], 1)
                        pe.wait_ge(s["gselT_act"], n + 1)
                        for k in range(4):
                            t, c = k // 2, k % 2
                            if k == 0:
                                pe.wait_ge(s["o_act"], n + 1 + FREE)
                            if k == 1:
                                pe.wait_ge(s["o_dve"], n + 1 + FREE)
                            pe.wait_ge(s["x_dve"], n * 4 + max(k - 1, 0) + X_FREE)
                            mm(bank(6 + k % 2), gselT[:, t * P:(t + 1) * P], o_sb[:, c * 512:(c + 1) * 512],
                               start=True, stop=True).then_inc(s["y2_psum"], 1)

        @block.scalar
        def _(act):
            af = nc.scalar.activation

            def conv(L, b):
                ch = uT_block(b)
                act.wait_ge(s["proj_psum"], L * 24 + b + 1)
                af(uT[:, ch], bank(b % 2, S), ACT.Identity, bias=vec[:, V_CB + ch:V_CB + ch + 1],
                   scale=vec[:, V_CW + 24 + ch:V_CW + 25 + ch]).then_inc(s["conv_act"], 1)

            def load_sqrt_table():
                af(small[:, 339:340], small[:, 338:339], ACT.Sqrt)

            eps = cst[:, C_EPS:C_EPS + 1]
            act.wait_ge(s["one_dve"], 1)
            for n in ("sil_act", "o_act"):
                act.sem_inc(s[n], FREE)
            with act.Fori(0, DEPTH) as L:
                load_sqrt_table()
                act.wait_ge(s["x_dve"], L * E * 4 + X_FREE - 2)
                act.dma_start(w12, filt12[L]).then_inc(s["filt_in"], 16)
                act.dma_start(w3, filt3[L]).then_inc(s["filt_in"], 16)
                act.wait_ge(s["x_in"], 16)
                for t in range(SB):
                    if t == 1:
                        act.wait_ge(s["x_dve"], L * E * 4 + X_FREE)
                    af(W[:, t * D:(t + 1) * D], x3[:, t], ACT.Square, accum_out=n1[:, t:t + 1])
                act.wait_ge(s["consts_in"], 16)
                act.drain()
                af(n1[:, 2:4], n1[:, 0:2], ACT.Sqrt, bias=eps, scale=1.0 / D).then_inc(s["norm1_rms"], 1)
                act.wait_ge(s["vec_in"], 16 * (L + 1))
                for b in (1, 3):
                    act.wait_ge(s["xnT_psum"], L * 4 + b + 1)
                    for i in (2 * b, 2 * b + 1):
                        m = af(xnT[:, i], bank(b, S, (i % 2) * S), ACT.Copy, scale=vec[:, V_N1 + i:V_N1 + i + 1])
                    m.then_inc(s["xnT_act"], 1)
                act.wait_ge(s["lat_psum"], L + 1)
                for t in range(SB):
                    af(uT_t[:, t * KSC:t * KSC + QR], bank(3 + 2 * t, QR), ACT.Square, accum_out=lr[:, t:t + 1])
                    af(uT_t[:, t * KSC + QR:t * KSC + QR + KVR], bank(4 + 2 * t, KVR), ACT.Square,
                       accum_out=lr[:, 2 + t:3 + t])
                act.drain()
                af(lr[:, 4:6], lr[:, 0:2], ACT.Sqrt, bias=eps, scale=1.0 / QR)
                af(lr[:, 6:8], lr[:, 2:4], ACT.Sqrt, bias=eps, scale=1.0 / KVR).then_inc(s["lat_rms"], 1)
                conv(L, 0)
                act.wait_ge(s["latT_psum"], L * 3 + 2)
                af(latT[:, 2], bank(3, S), ACT.Copy, scale=vec[:, V_QA + 2:V_QA + 3])
                af(latT[:, 3], bank(3, S, S), ACT.Copy, scale=vec[:, V_KVA:V_KVA + 1]).then_inc(s["latT_act"], 1)
                conv(L, 1)
                act.wait_ge(s["arg_dve"], 2 * L + 1)
                af(h1T, rr[:, 2 * S:3 * S], ACT.Sin).then_inc(s["sin_act"], 1)
                qsq_flat = uT_t[:, 3072:6144]
                for g in range(6):
                    t, c = g // 3, g % 3
                    act.wait_ge(s["q_psum"], L * 6 + g + 1)
                    af(qsq_flat[:, g * 512:(g + 1) * 512], bank((3 + g) % 7), ACT.Square)
                    af(q_t[:, t, c * 512:(c + 1) * 512], bank((3 + g) % 7), ACT.Copy).then_inc(s["q_act"], 1)
                    if g == 3:
                        act.wait_ge(s["arg_dve"], 2 * L + 2)
                        af(h2T, rr[:, 2 * S:3 * S], ACT.Sin).then_inc(s["sin_act"], 1)
                for t in range(SB):
                    act.wait_ge(s["kv_dve"], L * 8 + 4 * t + 2)
                    af(ksq[:, t], k4[:, t, :, 0:NOPE], ACT.Square).then_inc(s["ksq_act"], 1)
                act.wait_ge(s["qkss_dve"], L + 1)
                af(rqk[:, :], ssqk[:, :], ACT.Sqrt, bias=eps, scale=1.0 / QK).then_inc(s["qkrms_act"], 1)
                blocks = iter(range(2, 24))
                for _ in range(6):
                    conv(L, next(blocks))
                for h in range(NH + 1):
                    if h < NH:
                        act.wait_ge(s["qkT_psum"], L * NH + h + 1)
                        af(qkT[0:QK, h % 2], bank(2, rows=QK), ACT.Copy).then_inc(s["qkT_act"], 1)
                        act.wait_ge(s["max_dve"], L * NH + h + 1)
                        for t in range(SB):
                            c = 2 * (h % 2) + t
                            m = af(p_t[:, h % 2, t], bank(3 + h % 2, S, t * S), ACT.Exp, bias=nmax[:, c:c + 1],
                                   accum_out=rsum[:, c:c + 1])
                        m.then_inc(s["exp_act"], 1)
                        conv(L, next(blocks))
                    if h >= 1 and h % 2 == 0:
                        g = h - 1
                        act.wait_ge(s["pv_psum"], L * NH + g + 1)
                        af(aT[:, g // 2], bank(7, S), ACT.Copy).then_inc(s["oT_act"], 1)
                def sigmoids(i, dst, b):
                    act.wait_ge(s["gate_psum"], L * 8 + i + 1)
                    af(dst, bank(b), ACT.Sigmoid).then_inc(s["sig_act"], 1)

                act.dma_start(decay, decay_in).then_inc(s["decay_in"], 16)
                sigmoids(0, sg_early[:, 0], 2)
                def abs_h(it):
                    act.wait_ge(s["h_dve"], L * 4 + it + 1)
                    if it >= 1:
                        act.wait_ge(s["hsum_psum"], L * 4 + it)
                    af(habs, W[:, 2048:3072], ACT.Abs).then_inc(s["habs_act"], 1)

                abs_h(0)
                for it in range(4):
                    n, c = it // 2, it % 2
                    if it < 3:
                        abs_h(it + 1)
                    act.wait_ge(s["spec_dve"], L * 16 + 4 * it + 1)
                    cs = slice(c * HW, (c + 1) * HW)
                    af(spec[0:64, n, 3, cs], spec[64:128, n, 2, cs], ACT.Copy)
                    af(spec[64:128, n, 3, cs], spec[0:64, n, 2, cs], ACT.Copy).then_inc(s["swap_act"], 1)

                def z_out(it):
                    act.wait_ge(s["zT_psum"], L * 4 + it + 1)
                    for t in range(SB):
                        m = af(z_t[:, it % 2, t], bank(t), ACT.Copy)
                    m.then_inc(s["z_act"], 1)

                z_out(0)
                z_out(1)
                for it in range(4):
                    if it >= 2:
                        z_out(it)
                    act.wait_ge(s["prod_dve"], L * 4 + it + 1)
                    af(prod2[0:64, 2], prod2[64:128, 0], ACT.Copy)
                    af(prod2[64:128, 2], prod2[0:64, 1], ACT.Copy).then_inc(s["shift_act"], 1)
                    if it >= 1:
                        sigmoids(it, sg_early[:, it], 7)
                for i in range(4, DB):
                    if i >= 6:
                        act.wait_ge(s["merged_dve"], L * 8 + i - 1)
                    sigmoids(i, sg[:, i % 2], 2 * (i % 2))
                def squares(c):
                    act.wait_ge(s["xmid_dve"], L * 4 + 2 * c + 2)
                    for t in range(SB):
                        af(W[:, t * HW:(t + 1) * HW], x3[:, t, c * HW:(c + 1) * HW], ACT.Square,
                           accum_out=(n2, n2b)[c][:, t:t + 1])
                    act.drain()

                def scaled_copies(b):
                    act.wait_ge(s["xn2T_psum"], L * 4 + b + 1)
                    for i in (2 * b, 2 * b + 1):
                        m = af(aT[:, i], bank(b, S, (i % 2) * S), ACT.Copy, scale=fvec[:, W_N2 + i:W_N2 + i + 1])
                    m.then_inc(s["xn2T_act"], 1)

                load_sqrt_table()
                squares(0)
                act.wait_ge(s["fvec_in"], 16 * (L + 1))
                af(n2[:, 2:4], n2[:, 0:2], ACT.Identity, bias=eps, scale=1.0 / D)
                scaled_copies(1)
                squares(1)
                scaled_copies(3)
                for t in range(SB):
                    m = af(n2[:, 2 + t:3 + t], n2b[:, t:t + 1], ACT.Sqrt, bias=n2[:, 2 + t:3 + t], scale=1.0 / D)
                m.then_inc(s["norm2_rms"], 1)
                act.wait_ge(s["lmax_dve"], L + 1)
                for t in range(SB):
                    m = af(aff[:, t], bank(5, E, t * E), ACT.Exp, bias=lmax[:, t:t + 1],
                           scale=n2[:, t:t + 1], accum_out=lmax[:, 2 + t:3 + t])
                m.then_inc(s["lexp_act"], 1)
                for t in range(SB):
                    m = af(xn2[:, t], x3[:, t], ACT.Copy, scale=n2[:, t:t + 1])
                m.then_inc(s["xn2_act"], 1)
                with act.Fori(0, E) as e:
                    n = L * E + e
                    act.wait_ge(s["gate_done"], n + 1 + FREE)
                    act.wait_ge(s["hid_dve"], n + FREE)
                    af(sil, bank(2, FT), ACT.Silu).then_inc(s["sil_act"], 1)
                    act.wait_ge(s["gselT_psum"], n + 1)
                    af(gselT, bank(4, S), ACT.Copy).then_inc(s["gselT_act"], 1)
                    act.wait_ge(s["o_psum"], n + 1 + FREE)
                    af(o_sb[:, 0:512], bank(0), ACT.Copy).then_inc(s["o_act"], 1)

        @block.vector
        def _(dve):
            tt, ts, stt = nc.vector.tensor_tensor, nc.vector.tensor_scalar, nc.vector.scalar_tensor_tensor
            recip, copy, reduce = nc.vector.reciprocal, nc.vector.tensor_copy, nc.vector.tensor_reduce

            def conv(L, b):
                ch = uT_block(b)
                dve.wait_ge(s["conv_act"], L * 24 + b + 1)
                pb = b % 2
                stt(uT[:, ch, 1:S], bank(pb, S - 1), vec[:, V_CW + ch:V_CW + ch + 1], uT[:, ch, 1:S],
                    ALU.mult, ALU.add)
                dve.drain()
                stt(uT[:, ch, 0:S - 1], bank(pb, S - 1, 1), vec[:, V_CW + 48 + ch:V_CW + 49 + ch],
                    uT[:, ch, 0:S - 1], ALU.mult, ALU.add).then_inc(s["conv_dve"], 1)

            def sine_argument(L, k):
                dve.wait_ge(s["filt_psum"], 2 * L + k + 1)
                a, turns, rest = (rr[:, i * S:(i + 1) * S] for i in range(3))
                c = V_FB1 + 2 * k
                ts(a, bank(7, S, rows=64), vec[0:64, c:c + 1], vec[0:64, c + 1:c + 2], ALU.add, ALU.mult)
                dve.drain()
                ts(turns, a, 1.0 / TWO_PI, ROUND, ALU.mult, ALU.add)
                dve.drain()
                ts(turns, turns, ROUND, None, ALU.subtract)
                dve.drain()
                src = a
                for part in TWO_PI_PARTS:
                    stt(rest, turns, -part, src, ALU.mult, ALU.add)
                    dve.drain()
                    src = rest
                ts(rest, rest, PI_BELOW, -PI_BELOW, ALU.min, ALU.max).then_inc(s["arg_dve"], 1)

            def rope(T, A, B, cos, sin, swap=None):
                tt(A, T, cos, ALU.mult)
                tt(B[:, :, 0], T[:, :, 1], sin, ALU.mult)
                tt(B[:, :, 1], T[:, :, 0], sin, ALU.mult)
                dve.drain()
                tt(T[:, :, 0], A[:, :, 0], B[:, :, 0], ALU.subtract)
                tt(T[:, :, 1], A[:, :, 1], B[:, :, 1], ALU.add)

            nc.vector.memset(small[:, 338:339], 1.0).then_inc(s["one_dve"], 1)
            for n in ("post_dve", "xs_dve", "hid_dve", "o_dve"):
                dve.sem_inc(s[n], FREE)
            dve.sem_inc(s["x_dve"], X_FREE)
            with dve.Fori(0, DEPTH) as L:
                dve.wait_ge(s["norm1_rms"], L + 1)
                recip(n1[:, 0:2], n1[:, 2:4])
                dve.drain()
                for t in range(SB):
                    m = ts(xn[:, t], x3[:, t], n1[:, t:t + 1], None, ALU.mult)
                m.then_inc(s["xn_ready"], 1)
                dve.wait_ge(s["vec_in"], 16 * (L + 1))
                for b in (0, 2):
                    dve.wait_ge(s["xnT_psum"], L * 4 + b + 1)
                    for i in (2 * b, 2 * b + 1):
                        m = ts(xnT[:, i], bank(b, S, (i % 2) * S), vec[:, V_N1 + i:V_N1 + i + 1], None, ALU.mult)
                    m.then_inc(s["xnT_dve"], 1)
                dve.wait_ge(s["qkw_in"], 16 * (L + 1))
                ts(qkw[:, 0:QK], qkw[:, 0:QK], QK ** -0.5, None, ALU.mult).then_inc(s["qkw_scaled"], 1)
                dve.wait_ge(s["lat_rms"], L + 1)
                recip(lr[:, 0:4], lr[:, 4:8])
                dve.drain()
                for t in range(SB):
                    ts(lat[:, t, 0:QR], bank(3 + 2 * t, QR), lr[:, t:t + 1], None, ALU.mult)
                    copy(lat[:, t, QR:QR + ROPE], bank(3 + 2 * t, ROPE, QR))
                    m = ts(lat[:, t, QR + ROPE:LAT], bank(4 + 2 * t, KVR), lr[:, 2 + t:3 + t], None, ALU.mult)
                m.then_inc(s["lat_ready"], 1)
                dve.wait_ge(s["latT_psum"], L * 3 + 1)
                for i in (0, 1):
                    m = ts(latT[:, i], bank(2, S, i * S), vec[:, V_QA + i:V_QA + i + 1], None, ALU.mult)
                m.then_inc(s["latT_dve"], 1)
                dve.wait_ge(s["latT_psum"], L * 3 + 3)
                ts(latT[:, 4], bank(4, S), vec[:, V_KVA + 1:V_KVA + 2], None, ALU.mult).then_inc(s["latT_dve"], 1)
                conv(L, 0)
                conv(L, 1)
                sine_argument(L, 0)
                dve.wait_ge(s["consts_in"], 16)
                kraw = lat[:, :, QR:QR + ROPE]
                kr2 = small[:, 140:204].rearrange("p (b c) -> p b c", b=SB)
                krA2 = small[:, 204:268].rearrange("p (b c) -> p b c", b=SB)
                tt(krA2, kraw, kraw, ALU.mult)
                tt(kr2, kraw, qkw[:, QK + NOPE:2 * QK].unsqueeze(1).to_broadcast([P, SB, ROPE]), ALU.mult)
                dve.drain()
                reduce(kss, krA2, AX.X, ALU.add)
                dve.drain()
                cos2 = cst[:, C_COS:C_COS + SB * HALF].rearrange("p (b c) -> p b c", b=SB)
                sin2 = cst[:, C_SIN:C_SIN + SB * HALF].rearrange("p (b c) -> p b c", b=SB)
                rope(kr, krA, krB, cos2.unsqueeze(2).to_broadcast([P, SB, 2, HALF]), sin2)
                sine_argument(L, 1)
                for g in range(8):
                    t, c = g // 4, g % 4
                    dve.wait_ge(s["kv_psum"], L * 8 + g + 1)
                    src = bank((3 + g % 6) % 7)
                    if c < 2:
                        m = copy(k4[:, t, 8 * c:8 * c + 8, 0:NOPE], src.rearrange("p (h c) -> p h c", h=8))
                    else:
                        m = copy(v_t[:, t, (c - 2) * 512:(c - 1) * 512], src)
                    m.then_inc(s["kv_dve"], 1)
                    if 1 <= g < 5:
                        dve.wait_ge(s["q_act"], L * 6 + (3 if g < 3 else 6))
                        r = 8 * (g - 1)
                        reduce(ssqk[:, r:r + 8], qsq_rows[:, r:r + 8], AX.X, ALU.add)
                for t in range(SB):
                    r = NH * t
                    dve.wait_ge(s["ksq_act"], L * 2 + t + 1)
                    reduce(ssqk[:, 32 + r:48 + r], ksq_rows[:, r:r + NH], AX.X, ALU.add)
                dve.drain()
                for t in range(SB):
                    c = slice(32 + 16 * t, 48 + 16 * t)
                    m = ts(ssqk[:, c], ssqk[:, c], kss[:, t:t + 1], None, ALU.add)
                m.then_inc(s["qkss_dve"], 1)
                dve.wait_ge(s["qkrms_act"], L + 1)
                recip(rqk[:, :], rqk[:, :]).then_inc(s["rqk_dve"], 1)
                dve.drain()
                for t in range(SB):
                    conv(L, 2 + 2 * t)
                    rk = rqk[:, 32 + 16 * t:48 + 16 * t]
                    if t == 0:
                        dve.wait_ge(s["qw_pool"], L * 2 + 1)
                        tt(q4[:, 0], q4[:, 0], rqk[:, 0:NH].unsqueeze(2).to_broadcast([P, NH, QK]), ALU.mult)
                        dve.wait_ge(s["kw_pool"], L * 2 + 1)
                        tt(k4[:, 0, :, 0:NOPE], k4[:, 0, :, 0:NOPE], rk.unsqueeze(2).to_broadcast([P, NH, NOPE]),
                           ALU.mult)
                    conv(L, 3 + 2 * t)
                    tt(k4[:, t, :, NOPE:QK], kr2[:, t].unsqueeze(1).to_broadcast([P, NH, ROPE]),
                       rk.unsqueeze(2).to_broadcast([P, NH, ROPE]), ALU.mult)
                    if t == 1:
                        dve.wait_ge(s["qkr_pool"], L * 2 + 1)
                    rope(q4[:, t, :, NOPE:QK].rearrange("p h (t c) -> p h t c", t=2), rpA, rpB,
                         cos2[:, t].unsqueeze(1).unsqueeze(1).to_broadcast([P, NH, 2, HALF]),
                         sin2[:, t].unsqueeze(1).to_broadcast([P, NH, HALF]))
                    dve.drain()
                nc.vector.tensor_copy(kt, kss).then_inc(s["qk_ready"], 1)
                conv(L, 6)
                conv(L, 7)
                blocks = iter(range(8, 24))
                for h in range(NH + 1):
                    g = h - 1
                    if h >= 1:
                        dve.wait_ge(s["exp_act"], L * NH + g + 1)
                        c = 2 * (g % 2)
                        recip(rsum[:, c:c + 2], rsum[:, c:c + 2])
                        dve.drain()
                        for t in range(SB):
                            m = ts(p_t[:, g % 2, t], p_t[:, g % 2, t], rsum[:, c + t:c + t + 1], None, ALU.mult)
                        m.then_inc(s["p_dve"], 1)
                    if h == NH:
                        conv(L, next(blocks))
                    if h < NH:
                        dve.wait_ge(s["score_psum"], L * NH + h + 1)
                        reduce(nmax[:, 2 * (h % 2):2 * (h % 2) + 2],
                               bank(3 + h % 2).rearrange("p (t k) -> p t k", t=SB), AX.X, ALU.max,
                               negate=True).then_inc(s["max_dve"], 1)
                    if h >= 1:
                        dve.wait_ge(s["pT_psum"], L * NH + g + 1)
                        copy(W[:, 1024 + 512 * (g % 2):1536 + 512 * (g % 2)], bank(5 + g % 2)).then_inc(s["pT_dve"], 1)
                    if h < NH - 1:
                        conv(L, next(blocks))
                def decayed(it):
                    if it == 0:
                        dve.wait_ge(s["decay_in"], 16 * (L + 1))
                    else:
                        dve.wait_ge(s["dft_psum"], L * 12 + 3 * it)
                        dve.wait_ge(s["habs_act"], L * 4 + it)
                    dve.wait_ge(s["f3_psum"], L * 4 + it + 1)
                    c = it % 2
                    for t in range(SB):
                        m = tt(hflt[:, t], bank(2 * (it % 2) + t), decay[:, t, c * HW:(c + 1) * HW], ALU.mult)
                    m.then_inc(s["h_dve"], 1)

                decayed(0)
                for it in range(4):
                    n, c = it // 2, it % 2
                    cs = slice(c * HW, (c + 1) * HW)
                    for k, f in enumerate((2, 0, 1)):
                        if k == 2 and it < 3:
                            decayed(it + 1)
                        dve.wait_ge(s["dft_psum"], L * 12 + 3 * it + k + 1)
                        copy(spec[:, n, f, cs], bank(5 + f)).then_inc(s["spec_dve"], 1)
                    dve.wait_ge(s["hsum_psum"], L * 4 + it + 1)
                    k = n * DB + 4 * c
                    copy(hsum[:, k:k + 4], bank(4, 4)).then_inc(s["spec_dve"], 1)
                    dve.drain()
                    recip(hinv[:, k:k + 4], hsum[:, k:k + 4])
                    tt(hskip[:, k:k + 4], hsum[:, k:k + 4], vec[:, V_SKIP + k:V_SKIP + k + 4], ALU.mult)
                    dve.drain()

                def products(it):
                    n, c = it // 2, it % 2
                    cs = slice(c * HW, (c + 1) * HW)
                    dve.drain()
                    dve.wait_ge(s["zf_psum"], L * 12 + 3 * it + 1)
                    dve.wait_ge(s["swap_act"], L * 4 + it + 1)
                    sp_ = [spec[:, n, f, cs] for f in range(4)]
                    tt(prod[:, 0], bank(2), sp_[0], ALU.mult)
                    tt(prod[:, 2], bank(2), sp_[1], ALU.mult)
                    dve.wait_ge(s["zf_psum"], L * 12 + 3 * it + 2)
                    tt(prod[:, 1], bank(3), sp_[1], ALU.mult)
                    tt(prod[:, 3], bank(3), sp_[0], ALU.mult)
                    dve.wait_ge(s["zf_psum"], L * 12 + 3 * it + 3)
                    tt(prod2[:, 0], bank(4), sp_[2], ALU.mult)
                    tt(prod2[:, 1], bank(4), sp_[3], ALU.mult).then_inc(s["prod_dve"], 1)

                def spectrum(it):
                    dve.drain()
                    if it >= 1:
                        dve.wait_ge(s["y_psum"], L * 8 + 2 * it)
                    tt(yT_t[:, 0], prod[:, 0], prod[:, 1], ALU.subtract)
                    tt(yT_t[:, 1], prod[:, 2], prod[:, 3], ALU.add)
                    dve.wait_ge(s["shift_act"], L * 4 + it + 1)
                    tt(yT_t[0:64, 2], prod2[0:64, 0], prod2[0:64, 2], ALU.subtract)
                    tt(yT_t[64:128, 2], prod2[64:128, 1], prod2[64:128, 2], ALU.add).then_inc(s["yf_dve"], 1)

                def gate_z(it):
                    n, c = it // 2, it % 2
                    for jj in range(2):
                        dve.wait_ge(s["y_psum"], L * 8 + 2 * it + jj + 1)
                        b0 = 4 * c + 2 * jj
                        for r in range(2):
                            k = n * DB + b0 + r
                            stt(uT[:, b0 + r], uT[:, b0 + r], hskip[:, k:k + 1], bank(5 + jj, S, r * S),
                                ALU.mult, ALU.add)
                        dve.drain()
                        for r in range(2):
                            k = n * DB + b0 + r
                            m = stt(uT[:, b0 + r], uT[:, b0 + r], hinv[:, k:k + 1], uT[:, 8 * (n + 1) + b0 + r],
                                    ALU.mult, ALU.mult)
                    m.then_inc(s["post_dve"], 1)

                products(0)
                spectrum(0)
                for it in range(4):
                    if it < 3:
                        products(it + 1)
                    gate_z(it)
                    if it < 3:
                        spectrum(it + 1)
                for i in range(DB):
                    dve.wait_ge(s["sig_act"], L * 8 + i + 1)
                    dve.wait_ge(s["branch_psum"], L * 8 + i + 1)
                    gm = gm_t[:, i % 2]
                    tt(gm, sg[:, i % 2] if i >= 4 else sg_early[:, i], bank(2 * (i % 2) + 1), ALU.mult)
                    dve.drain()
                    tt(mT[:, i], gm[:, 0:S], gm[:, S:2 * S], ALU.add).then_inc(s["merged_dve"], 1)
                for k in range(4):
                    c, t = k // 2, k % 2
                    dve.wait_ge(s["wout_psum"], L * 4 + k + 1)
                    xc = x3[:, t, c * 512:(c + 1) * 512]
                    tt(xc, xc, bank(4 + k), ALU.add).then_inc(s["xmid_dve"], 1)
                dve.wait_ge(s["fvec_in"], 16 * (L + 1))
                for b in (0, 2):
                    dve.wait_ge(s["xn2T_psum"], L * 4 + b + 1)
                    for i in (2 * b, 2 * b + 1):
                        m = ts(aT[:, i], bank(b, S, (i % 2) * S), fvec[:, W_N2 + i:W_N2 + i + 1], None, ALU.mult)
                    m.then_inc(s["xn2T_dve"], 1)
                dve.wait_ge(s["norm2_rms"], L + 1)
                recip(n2[:, 0:2], n2[:, 2:4])
                dve.wait_ge(s["lgT_psum"], L + 1)
                copy(lgT, bank(4, S, rows=E)).then_inc(s["lgT_dve"], 1)
                dve.wait_ge(s["lg_psum"], L + 1)
                reduce(lmax[:, 0:2], bank(5, SB * E).rearrange("p (t e) -> p t e", t=SB), AX.X, ALU.max,
                       negate=True)
                dve.drain()
                tt(lmax[:, 0:2], lmax[:, 0:2], n2[:, 0:2], ALU.mult).then_inc(s["lmax_dve"], 1)
                dve.wait_ge(s["lexp_act"], L + 1)
                recip(lmax[:, 2:4], lmax[:, 2:4])
                dve.drain()
                for t in range(SB):
                    m = ts(aff[:, t], aff[:, t], lmax[:, 2 + t:3 + t], None, ALU.mult)
                m.then_inc(s["aff_dve"], 1)
                dve.wait_ge(s["affT_psum"], L + 1)
                copy(work, bank(6, S, rows=E))
                dve.drain()
                for _ in range(CAP // 8):
                    nc.vector.max(top8, work)
                    dve.drain()
                    nc.vector.match_replace(work, top8, work, -1.0)
                    dve.drain()
                ts(picked, work, 0.0, None, ALU.is_lt)
                dve.drain()
                nc.vector.tensor_tensor_scan(rank, picked, picked, 0.0, ALU.add, ALU.max)
                dve.drain()
                tt(ptok, rank, picked, ALU.mult).then_inc(s["pos_dve"], 1)
                dve.wait_ge(s["pos_psum"], L + 1)
                copy(pos_flat, bank(7, SB * E))
                dve.drain()

                with dve.Fori(0, NG) as g:
                    for t in range(SB):
                        m = tt(pick[:, t].rearrange("p (q c) -> p q c", q=GROUP),
                               cst[:, C_IOTA:C_IOTA + P].rearrange("p (q c) -> p q c", q=GROUP),
                               pos[:, t, ds(g * GROUP, GROUP)].unsqueeze(2).to_broadcast([P, GROUP, CAP]),
                               ALU.is_equal)
                    m.then_inc(s["pick_dve"], 1)
                    for b in range(2):
                        dve.wait_ge(s["xs_psum"], 2 * (L * NG + g) + b + 1)
                        m = tt(xs[:, 4 * b:4 * b + 4], bank(b).rearrange("p (i c) -> p i c", i=4),
                               fvec[:, W_N2 + 4 * b:W_N2 + 4 * b + 4].unsqueeze(2).to_broadcast([P, 4, P]),
                               ALU.mult)
                    m.then_inc(s["xs_dve"], 1)
                    for q in range(GROUP):
                        e = g * GROUP + q
                        n = L * E + e
                        for t in range(SB):
                            m = ts(gsel[:, t], cst[:, C_IOTA:C_IOTA + P], pos[:, t, ds(e, 1)],
                                   aff[:, t, ds(e, 1)], ALU.is_equal, ALU.mult)
                        m.then_inc(s["gsel_dve"], 1)
                        dve.wait_ge(s["sil_act"], n + 1 + FREE)
                        dve.wait_ge(s["up_done"], n + 1 + FREE)
                        tt(hid_e, sil, bank(3, FT), ALU.mult).then_inc(s["hid_dve"], 1)
                        dve.wait_ge(s["hT_psum"], n + 1)
                        copy(hT[:, 0:2 * P], bank(5, 2 * P))
                        copy(hT[0:KF[2], 2 * P:3 * P], bank(5, P, 2 * P, rows=KF[2])).then_inc(s["hT_dve"], 1)
                        dve.wait_ge(s["o_psum"], n + 1 + FREE)
                        copy(o_sb[:, 512:1024], bank(1)).then_inc(s["o_dve"], 1)
                        for k in range(4):
                            t, c = k // 2, k % 2
                            dve.wait_ge(s["y2_psum"], n * 4 + k + 1)
                            xc = x3[:, t, c * 512:(c + 1) * 512]
                            tt(xc, xc, bank(6 + k % 2), ALU.add).then_inc(s["x_dve"], 1)


def constants():
    import numpy as np
    k = np.arange(NF // 2)[:, None]
    th = np.pi * (2 * k + 1) / NF
    f = th * np.arange(S)[None, :]
    g = th * (np.arange(S)[None, :] + S // 2)
    cf, sf, ci, si = np.cos(f), -np.sin(f), 2 / NF * np.cos(g), -2 / NF * np.sin(g)
    fwd = np.concatenate([cf[:P], sf[:P], cf[P:], sf[P:]])
    inv = np.concatenate([ci[:P], si[:P], ci[P:], si[P:]])
    c = np.zeros((P, C_N), np.float32)
    c[:, C_ID:C_ID + P] = np.eye(P)
    c[:, C_F:C_F + SB * NF] = fwd.T.reshape(SB, P, NF).transpose(1, 0, 2).reshape(P, -1)
    c[:, C_IF:C_IF + 3 * S] = inv.reshape(3, P, S).transpose(1, 0, 2).reshape(P, -1)
    f32 = np.float32
    inv_freq = f32(10000.0) ** (-np.arange(0, ROPE, 2, dtype=f32) / f32(ROPE))
    ang = (np.arange(S, dtype=f32)[:, None] * inv_freq[None]).astype(f32)
    for at, tab in ((C_COS, np.cos(ang)), (C_SIN, np.sin(ang))):
        c[:, at:at + SB * HALF] = tab.reshape(SB, P, HALF).transpose(1, 0, 2).reshape(P, -1)
    c[:, C_IOTA:C_IOTA + P] = np.arange(P)[None] % CAP + 1
    c[:, C_ONES] = 1.0
    pos = np.arange(S, dtype=f32)
    tm = pos / f32(S)
    bands = 16
    w = f32(2.0 * np.pi) * tm[:, None] * np.linspace(1e-4, bands - 1, bands, dtype=f32)[None]
    feats = np.concatenate([tm[:, None], np.cos(w), np.sin(w)], -1)
    c[0:33, C_FEAT:C_FEAT + S] = feats.T
    c[:, C_EPS] = EPS
    tau = np.abs(pos - S // 2) / f32(S // 2)
    low, high = np.log(1e-2) / 1.5, np.log(1e-2) / 0.3
    delta = np.abs(np.linspace(low, high, D, dtype=f32))
    decay = np.exp(-tau[:, None] * delta[None]).astype(f32)
    decay = np.ascontiguousarray(decay.reshape(SB, P, D).transpose(1, 0, 2))
    return c, decay


def kernel(**inputs):
    import concourse.bacc as bacc
    import numpy as np
    from concourse.bass_utils import run_bass_kernel_spmd

    a = {k: np.asarray(v) for k, v in inputs.items()}

    def cols(v):
        return v.reshape(DEPTH, -1, P).transpose(0, 2, 1)

    def k_major(w):
        return w.reshape(DEPTH, -1, P, w.shape[-1]).transpose(0, 2, 1, 3)

    small = np.zeros((DEPTH, P, 4), np.float32)
    for i, name in enumerate(("filt_b1", "filt_freq1", "filt_b2", "filt_freq2")):
        small[:, 0:64, i] = a[name]
    vecs = np.concatenate([cols(a["norm1_w"]), cols(a["q_a_norm_w"]), cols(a["kv_a_norm_w"]),
                           cols(a["short_conv_w"].reshape(DEPTH, -1)), cols(a["short_conv_b"]),
                           cols(a["filt_skip"].reshape(DEPTH, -1)), small], 2)
    fvecs = np.concatenate([cols(a["norm2_w"]), k_major(a["router_w"]).reshape(DEPTH, P, -1)], 2)
    qkw = np.concatenate([a["q_norm_w"], a["k_norm_w"]], 1)
    w_in = k_major(a["w_in"])
    kv0, rope0, hy0 = QR, QR + KVR, QR + KVR + ROPE
    gate0 = hy0 + 3 * D
    w_lat = np.concatenate([w_in[..., 0:QR], w_in[..., rope0:hy0], w_in[..., kv0:rope0]], 3).reshape(DEPTH, P, -1)
    w_kv = k_major(a["w_kv_b"]).reshape(DEPTH, P, KVB, NH, 2, NOPE).transpose(0, 1, 2, 4, 3, 5)
    units = [w_kv.reshape(DEPTH, P, UNIT)]

    def half(w, c0):
        return w[..., c0:c0 + HW].reshape(DEPTH, P, UNIT)

    w_a, w_h, w_o = k_major(a["w_attn_branch"]), k_major(a["w_hyena_branch"]), k_major(a["w_out"])
    for c in range(2):
        units += [half(w_in, hy0 + p * D + c * HW) for p in range(3)]
    for c in range(2):
        units += [half(w_in, gate0 + c * HW), half(w_in, gate0 + D + c * HW), half(w_a, c * HW), half(w_h, c * HW)]
    units += [half(w_o, 0), half(w_o, HW)]
    filt12 = np.zeros((DEPTH, 64, 192), np.float32)
    filt12[:, 0:33, 0:64] = a["filt_w1"]
    filt12[:, :, 64:128] = a["filt_w2"]
    consts, decay = constants()
    feed = {
        "x_in": a["x"], "vecs": vecs, "fvecs": fvecs, "qkw": qkw, "consts": consts, "decay": decay,
        "w_lat": w_lat, "w_q_b": a["w_q_b"], "units": np.stack(units, 1), "filt12": filt12,
        "filt3": a["filt_w3"],
        "w_gate": a["expert_w_gate"].reshape(DEPTH * E, D, FF), "w_up": a["expert_w_up"].reshape(DEPTH * E, D, FF),
        "w_down": a["expert_w_down"].reshape(DEPTH * E, FF, D),
    }
    nc = bacc.Bacc("TRN2", target_bir_lowering=False, num_devices=1)
    arrays, args = {}, []
    for name, v in feed.items():
        v = np.ascontiguousarray(v)
        arrays[name + "_dram"] = v
        args.append(nc.dram_tensor(name + "_dram", v.shape, mybir.dt.from_np(v.dtype), kind="ExternalInput").ap())
    args.append(nc.dram_tensor("out_dram", (1, S, D), F32, kind="ExternalOutput").ap())
    build(nc, *args)
    r = run_bass_kernel_spmd(nc, [arrays], core_ids=[0])
    return r.results[0]["out_dram"]
```
